# Optimizing a Trainium2 kernel written in Bass

```python
import math
import jax, jax.numpy as jnp
from jax import lax
import numpy as np

D_MODEL = 1024
BATCH = 1
SEQ = 512
DEPTH = 1

MEM_LEN = 256
RMS_EPS = 1e-6
RW_HEADS = 8
RW_HEAD_DIM = 64
RW_WIDTH = RW_HEADS * RW_HEAD_DIM
DECAY_LORA = 64
AAA_LORA = 64
LNX_EPS = 64e-5
L2_EPS = 1e-12
SW_HEADS = 8
SW_KV_HEADS = 2
SW_GROUP = SW_HEADS // SW_KV_HEADS
SW_HEAD_DIM = 64
SW_WIDTH = SW_HEADS * SW_HEAD_DIM
SW_KV_WIDTH = SW_KV_HEADS * SW_HEAD_DIM
WINDOW = 128
BLOCK = 128
ROPE_THETA = 10000.0
NEG_INF = -1e30
X_HEADS = 4
X_HEAD_DIM = 128
X_WIDTH = X_HEADS * X_HEAD_DIM
N_BRANCHES = 3

IN_SPLITS = (RW_WIDTH, RW_WIDTH, RW_WIDTH, DECAY_LORA, AAA_LORA, RW_WIDTH,
             SW_WIDTH, SW_KV_WIDTH, SW_KV_WIDTH, SW_WIDTH,
             X_WIDTH, X_WIDTH,
             N_BRANCHES * D_MODEL)
IN_WIDTH = sum(IN_SPLITS)


def rms_norm(x, g):
    xf = x.astype(jnp.float32)
    y = xf * lax.rsqrt(jnp.mean(xf * xf, axis=-1, keepdims=True) + RMS_EPS)
    return (y * g.astype(jnp.float32)).astype(x.dtype)

def token_shift_mix(u, mu):
    prev = jnp.pad(u, ((0, 0), (1, 0), (0, 0)))[:, :-1]
    return u + (prev - u) * mu

def rope(x, pos):
    d = x.shape[-1]
    half = d // 2
    inv = ROPE_THETA ** (-jnp.arange(half, dtype=jnp.float32) / half)
    ang = pos.astype(jnp.float32)[..., None] * inv
    cos = jnp.cos(ang)[:, :, None, :]
    sin = jnp.sin(ang)[:, :, None, :]
    xf = x.astype(jnp.float32)
    x1, x2 = xf[..., :half], xf[..., half:]
    return jnp.concatenate([x1 * cos - x2 * sin, x2 * cos + x1 * sin], axis=-1).astype(x.dtype)

def rwkv7_scan(r, w, k, v, a, b):
    def step(S, inp):
        r_t, w_t, k_t, v_t, a_t, b_t = inp
        sa = jnp.einsum('bhvk,bhk->bhv', S, a_t)
        S = S * w_t[:, :, None, :] + sa[..., None] * b_t[:, :, None, :] + v_t[..., None] * k_t[:, :, None, :]
        y = jnp.einsum('bhvk,bhk->bhv', S, r_t)
        return S, y
    bsz, _, h, n = r.shape
    xs = tuple(jnp.moveaxis(t, 1, 0) for t in (r, w, k, v, a, b))
    s0 = jnp.zeros((bsz, h, n, n), jnp.float32)
    _, y = lax.scan(step, s0, xs)
    return jnp.moveaxis(y, 0, 1)

def rwkv7_mix(p_r, p_k, p_v, p_w, p_a, mu_rkv, mu_wa, w0, w2, a0, a2, k_k, k_a, r_k, lnx_g, lnx_b):
    f32 = jnp.float32
    bsz, t, _ = p_r.shape
    r = token_shift_mix(p_r, mu_rkv[0]).astype(f32)
    k = token_shift_mix(p_k, mu_rkv[1]).astype(f32)
    v = token_shift_mix(p_v, mu_rkv[2]).astype(f32)
    lw = token_shift_mix(p_w, mu_wa[0]).astype(f32)
    la = token_shift_mix(p_a, mu_wa[1]).astype(f32)
    w_log = -jax.nn.softplus(-(w0.astype(f32) + jnp.tanh(lw) @ w2.astype(f32))) - 0.5
    decay = jnp.exp(-jnp.exp(w_log))
    a = jax.nn.sigmoid(a0.astype(f32) + la @ a2.astype(f32))
    heads = lambda u: u.reshape(bsz, t, RW_HEADS, RW_HEAD_DIM)
    kk = heads(k * k_k.astype(f32))
    kk = kk / jnp.maximum(jnp.linalg.norm(kk, axis=-1, keepdims=True), L2_EPS)
    k = k * (1.0 + (a - 1.0) * k_a.astype(f32))
    rh, kh, vh, ah = heads(r), heads(k), heads(v), heads(a)
    y = rwkv7_scan(rh, heads(decay), kh, vh, -kk, kk * ah)
    mean = jnp.mean(y, axis=-1, keepdims=True)
    var = jnp.mean(jnp.square(y - mean), axis=-1, keepdims=True)
    y = ((y - mean) * lax.rsqrt(var + LNX_EPS)).reshape(bsz, t, RW_WIDTH) * lnx_g.astype(f32) + lnx_b.astype(f32)
    bonus = jnp.sum(rh * kh * r_k.astype(f32), axis=-1, keepdims=True) * vh
    return y + bonus.reshape(bsz, t, RW_WIDTH)

def sliding_window_sink_attn(q, k, v, pos, q_g, k_g, sinks):
    bsz, t, _ = q.shape
    nb = t // BLOCK
    q = rope(rms_norm(q.reshape(bsz, t, SW_HEADS, SW_HEAD_DIM), q_g), pos)
    k = rope(rms_norm(k.reshape(bsz, t, SW_KV_HEADS, SW_HEAD_DIM), k_g), pos)
    v = v.reshape(bsz, t, SW_KV_HEADS, SW_HEAD_DIM)
    qb = q.reshape(bsz, nb, BLOCK, SW_KV_HEADS, SW_GROUP, SW_HEAD_DIM)
    def band(u):
        ub = u.reshape(bsz, nb, BLOCK, SW_KV_HEADS, SW_HEAD_DIM)
        prev = jnp.pad(ub, ((0, 0), (1, 0), (0, 0), (0, 0), (0, 0)))[:, :-1]
        return jnp.concatenate([prev, ub], axis=2)
    kband, vband = band(k), band(v)
    scale = SW_HEAD_DIM ** -0.5
    s = jnp.einsum('bnqhgd,bnkhd->bnhgqk', qb, kband).astype(jnp.float32) * scale
    qi = jnp.arange(BLOCK)[:, None]
    kj = jnp.arange(2 * BLOCK)[None, :]
    rel = qi - kj + BLOCK
    allowed = (rel >= 0) & (rel < WINDOW)
    not_pad = (jnp.arange(nb)[:, None, None] > 0) | (kj >= BLOCK)[None]
    mask = allowed[None] & not_pad
    s = jnp.where(mask[None, :, None, None], s, NEG_INF)
    sink = jnp.broadcast_to(sinks.astype(jnp.float32).reshape(SW_KV_HEADS, SW_GROUP)[None, None, :, :, None, None],
                            s.shape[:-1] + (1,))
    p = jax.nn.softmax(jnp.concatenate([s, sink], axis=-1), axis=-1)[..., :-1]
    o = jnp.einsum('bnhgqk,bnkhd->bnqhgd', p.astype(v.dtype), vband)
    return o.reshape(bsz, t, SW_WIDTH)

def memory_cross_attn(q, mem, mem_norm_g, w_mem_kv, xq_g, xk_g):
    bsz, t, _ = q.shape
    m = mem.shape[1]
    q = rms_norm(q.reshape(bsz, t, X_HEADS, X_HEAD_DIM), xq_g)
    kv = rms_norm(mem, mem_norm_g) @ w_mem_kv
    km, vm = kv[..., :X_WIDTH], kv[..., X_WIDTH:]
    km = rms_norm(km.reshape(bsz, m, X_HEADS, X_HEAD_DIM), xk_g)
    vm = vm.reshape(bsz, m, X_HEADS, X_HEAD_DIM)
    s = jnp.einsum('bthd,bmhd->bhtm', q, km).astype(jnp.float32) * (X_HEAD_DIM ** -0.5)
    p = jax.nn.softmax(s, axis=-1)
    o = jnp.einsum('bhtm,bmhd->bthd', p.astype(vm.dtype), vm)
    return o.reshape(bsz, t, X_WIDTH)

def first_inputs(seed: int = 0) -> dict:
    key = jax.random.key(seed)
    ks = iter(jax.random.split(key, 40))
    f32 = jnp.float32
    def nrm(shape, scale):
        return jax.random.normal(next(ks), shape, f32) * scale
    L = DEPTH
    x = jax.random.normal(next(ks), (BATCH, SEQ, D_MODEL), f32)
    mem = jax.random.normal(next(ks), (BATCH, MEM_LEN, D_MODEL), f32)
    offset = jax.random.randint(next(ks), (BATCH, 1), 0, 4096, dtype=jnp.int32)
    positions = jnp.arange(SEQ, dtype=jnp.int32)[None, :] + offset
    return {
        'x': x,
        'mem': mem,
        'positions': positions,
        'norm_g': 1.0 + nrm((L, D_MODEL), 0.05),
        'mem_norm_g': 1.0 + nrm((L, D_MODEL), 0.05),
        'w_in': nrm((L, D_MODEL, IN_WIDTH), D_MODEL ** -0.5),
        'mu_rkv': jax.random.uniform(next(ks), (L, 3, RW_WIDTH), f32),
        'mu_wa': jax.random.uniform(next(ks), (L, 2, DECAY_LORA), f32),
        'w0': jnp.linspace(-6.0, -1.0, RW_WIDTH, dtype=f32)[None, :] + nrm((L, RW_WIDTH), 0.1),
        'w2': nrm((L, DECAY_LORA, RW_WIDTH), 0.5 * DECAY_LORA ** -0.5),
        'a0': nrm((L, RW_WIDTH), 0.1),
        'a2': nrm((L, AAA_LORA, RW_WIDTH), 0.5 * AAA_LORA ** -0.5),
        'k_k': 0.85 + nrm((L, RW_WIDTH), 0.05),
        'k_a': 1.0 + nrm((L, RW_WIDTH), 0.05),
        'r_k': nrm((L, RW_HEADS, RW_HEAD_DIM), 0.1),
        'lnx_g': 1.0 + nrm((L, RW_WIDTH), 0.05),
        'lnx_b': nrm((L, RW_WIDTH), 0.01),
        'q_norm_g': 1.0 + nrm((L, SW_HEAD_DIM), 0.05),
        'k_norm_g': 1.0 + nrm((L, SW_HEAD_DIM), 0.05),
        'sinks': nrm((L, SW_HEADS), 1.0),
        'xq_norm_g': 1.0 + nrm((L, X_HEAD_DIM), 0.05),
        'xk_norm_g': 1.0 + nrm((L, X_HEAD_DIM), 0.05),
        'w_mem_kv': nrm((L, D_MODEL, 2 * X_WIDTH), D_MODEL ** -0.5),
        'w_proj_a': nrm((L, RW_WIDTH, D_MODEL), RW_WIDTH ** -0.5),
        'w_proj_b': nrm((L, SW_WIDTH, D_MODEL), SW_WIDTH ** -0.5),
        'w_proj_c': nrm((L, X_WIDTH, D_MODEL), X_WIDTH ** -0.5),
        'w_out': nrm((L, D_MODEL, D_MODEL), D_MODEL ** -0.5),
    }

def first_block(x, mem, positions, norm_g, mem_norm_g, w_in, mu_rkv, mu_wa, w0, w2, a0, a2, k_k, k_a, r_k,
              lnx_g, lnx_b, q_norm_g, k_norm_g, sinks, xq_norm_g, xk_norm_g, w_mem_kv,
              w_proj_a, w_proj_b, w_proj_c, w_out):
    bsz, t, _ = x.shape
    split_points = [int(i) for i in np.cumsum(IN_SPLITS)[:-1]]
    for l in range(DEPTH):
        h = rms_norm(x, norm_g[l])
        p = h @ w_in[l]
        (p_r, p_k, p_v, p_w, p_a, z_a,
         p_q, p_sk, p_sv, z_b,
         p_xq, z_c, p_gate) = jnp.split(p, split_points, axis=-1)
        y_a = rwkv7_mix(p_r, p_k, p_v, p_w, p_a, mu_rkv[l], mu_wa[l], w0[l], w2[l], a0[l], a2[l],
                        k_k[l], k_a[l], r_k[l], lnx_g[l], lnx_b[l]).astype(x.dtype) * jax.nn.silu(z_a)
        y_b = sliding_window_sink_attn(p_q, p_sk, p_sv, positions, q_norm_g[l], k_norm_g[l],
                                       sinks[l]) * jax.nn.silu(z_b)
        y_c = memory_cross_attn(p_xq, mem, mem_norm_g[l], w_mem_kv[l], xq_norm_g[l],
                                xk_norm_g[l]) * jax.nn.silu(z_c)
        gates = jax.nn.sigmoid(p_gate.astype(jnp.float32)).reshape(bsz, t, N_BRANCHES, D_MODEL)
        merged = (gates[:, :, 0] * (y_a @ w_proj_a[l]) + gates[:, :, 1] * (y_b @ w_proj_b[l])
                  + gates[:, :, 2] * (y_c @ w_proj_c[l]))
        x = x + (merged.astype(x.dtype) @ w_out[l]).astype(x.dtype)
    return x


N_MEM = 256
A_HEADS = 8
HEAD_DIM = 64
A_WIDTH = A_HEADS * HEAD_DIM
IDX_HEADS = 4
IDX_DIM = 64
TOPK_MAX = 256
Q_BLOCK = 128
B_GROUPS = 8
B_WIDTH = D_MODEL - A_WIDTH
CONV_B_WIDTH = 31
MIX_WIDTH = A_WIDTH + B_WIDTH
ROPE_THETA_2 = 500000.0
ROT_DIM = HEAD_DIM // 4
CROSS_HEADS = 4
CROSS_HEAD_DIM = D_MODEL // CROSS_HEADS
D_FF = 2816
FFN_CONV_WIDTH = 3
EPS = 1e-6
IN_SPLITS_2 = (A_WIDTH, HEAD_DIM, HEAD_DIM, IDX_HEADS * IDX_DIM, IDX_DIM, IDX_HEADS, 2 * B_WIDTH)
IN_COLS = sum(IN_SPLITS_2)


def rmsnorm(x, g):
    xf = x.astype(jnp.float32)
    y = xf * lax.rsqrt(jnp.mean(xf * xf, axis=-1, keepdims=True) + EPS)
    return (y * g.astype(jnp.float32)).astype(x.dtype)

def layernorm(x, g, b):
    xf = x.astype(jnp.float32)
    mu = jnp.mean(xf, axis=-1, keepdims=True)
    var = jnp.mean(jnp.square(xf - mu), axis=-1, keepdims=True)
    y = (xf - mu) * lax.rsqrt(var + EPS)
    return (y * g.astype(jnp.float32) + b.astype(jnp.float32)).astype(x.dtype)

def causal_dwconv(x, w, b):
    width, ch = w.shape
    y = lax.conv_general_dilated(
        x, w.astype(x.dtype)[:, None, :], window_strides=(1,),
        padding=[(width - 1, 0)], dimension_numbers=('NWC', 'WIO', 'NWC'),
        feature_group_count=ch)
    return y + b.astype(x.dtype)

def rope_tables(positions):
    freqs = ROPE_THETA_2 ** (-jnp.arange(0, ROT_DIM, 2, dtype=jnp.float32) / ROT_DIM)
    ang = positions.astype(jnp.float32)[:, :, None, None] * freqs
    return jnp.cos(ang), jnp.sin(ang)

def partial_rope(x, cos, sin):
    xr = x[..., :ROT_DIM].astype(jnp.float32)
    x1, x2 = xr[..., :ROT_DIM // 2], xr[..., ROT_DIM // 2:]
    rot = jnp.concatenate([x1 * cos - x2 * sin, x2 * cos + x1 * sin], axis=-1)
    return jnp.concatenate([rot.astype(x.dtype), x[..., ROT_DIM:]], axis=-1)

def dsa_attention(q, k, v, qi, ki, wi):
    bsz, seq = q.shape[0], q.shape[1]
    nb = seq // Q_BLOCK
    topk = min(TOPK_MAX, seq // 4)
    qi = qi * (IDX_DIM ** -0.5)
    wi = wi * (IDX_HEADS ** -0.5)
    gather = jax.vmap(lambda a, i: a[i])
    key_pos = jnp.arange(seq)

    def block(args):
        bi, qb, qib, wib = args
        t = bi * Q_BLOCK + jnp.arange(Q_BLOCK)
        causal = key_pos[None, :] <= t[:, None]
        rel = jax.nn.relu(jnp.einsum('bqhd,bsd->bqhs', qib, ki).astype(jnp.float32))
        score = jnp.einsum('bqh,bqhs->bqs', wib.astype(jnp.float32), rel)
        score = jnp.where(causal[None], score, -jnp.inf)
        _, sel = lax.top_k(score, topk)
        k_sel = gather(k, sel)
        v_sel = gather(v, sel)
        valid = sel <= t[None, :, None]
        logits = jnp.einsum('bqhd,bqkd->bqhk', qb, k_sel).astype(jnp.float32) * (HEAD_DIM ** -0.5)
        logits = jnp.where(valid[:, :, None, :], logits, -jnp.inf)
        p = jax.nn.softmax(logits, axis=-1).astype(v.dtype)
        return jnp.einsum('bqhk,bqkd->bqhd', p, v_sel)

    to_blocks = lambda a: a.reshape(bsz, nb, Q_BLOCK, *a.shape[2:]).swapaxes(0, 1)
    out = lax.map(block, (jnp.arange(nb), to_blocks(q), to_blocks(qi), to_blocks(wi)))
    return out.swapaxes(0, 1).reshape(bsz, seq, A_WIDTH)

def hybrid_layer(x, mem, cos, sin, norm_mix_g, w_in, w_out, conv_b_w, conv_b_b, ln_b_g, ln_b_b,
                 norm_cross_g, norm_mem_g, w_q_cross, w_k_cross, w_v_cross, w_o_cross,
                 norm_ffn_g, w_gate, w_up, ffn_conv_w, ffn_conv_b, w_down):
    bsz, seq, _ = x.shape
    h = rmsnorm(x, norm_mix_g)
    proj = h @ w_in
    cuts = [int(c) for c in np.cumsum(IN_SPLITS_2)[:-1]]
    q, k, v, qi, ki, wi, glu = jnp.split(proj, cuts, axis=-1)
    q = partial_rope(q.reshape(bsz, seq, A_HEADS, HEAD_DIM), cos, sin)
    k = partial_rope(k[:, :, None, :], cos, sin)[:, :, 0]
    qi = partial_rope(qi.reshape(bsz, seq, IDX_HEADS, IDX_DIM), cos, sin)
    ki = partial_rope(ki[:, :, None, :], cos, sin)[:, :, 0]
    a_out = dsa_attention(q, k, v, qi, ki, wi)
    ga, gg = jnp.split(glu, 2, axis=-1)
    u = ga * jax.nn.sigmoid(gg)
    u = causal_dwconv(u, conv_b_w, conv_b_b)
    b_out = jax.nn.silu(layernorm(u, ln_b_g, ln_b_b))
    x = x + jnp.concatenate([a_out, b_out], axis=-1) @ w_out
    hq = rmsnorm(x, norm_cross_g)
    m = rmsnorm(mem, norm_mem_g)
    qc = (hq @ w_q_cross).reshape(bsz, seq, CROSS_HEADS, CROSS_HEAD_DIM)
    kc = (m @ w_k_cross).reshape(bsz, -1, CROSS_HEADS, CROSS_HEAD_DIM)
    vc = (m @ w_v_cross).reshape(bsz, -1, CROSS_HEADS, CROSS_HEAD_DIM)
    logits = jnp.einsum('bshd,bnhd->bhsn', qc, kc).astype(jnp.float32) * (CROSS_HEAD_DIM ** -0.5)
    p = jax.nn.softmax(logits, axis=-1).astype(vc.dtype)
    oc = jnp.einsum('bhsn,bnhd->bshd', p, vc).reshape(bsz, seq, D_MODEL)
    x = x + oc @ w_o_cross
    hf = rmsnorm(x, norm_ffn_g)
    g = causal_dwconv(hf @ w_gate, ffn_conv_w, ffn_conv_b)
    x = x + (jax.nn.silu(g) * (hf @ w_up)) @ w_down
    return x

def second_inputs(seed: int = 0) -> dict:
    key = jax.random.key(seed)
    ks = jax.random.split(key, 24)
    f32 = jnp.float32
    nrm = lambda k, shape, scale: jax.random.normal(k, shape, f32) * scale
    gain = lambda k, shape: 1.0 + 0.02 * jax.random.normal(k, shape, f32)
    L = DEPTH
    offsets = jax.random.randint(ks[2], (BATCH, 1), 0, 2048, dtype=jnp.int32)
    positions = offsets + jnp.arange(SEQ, dtype=jnp.int32)[None, :]
    return {
        'x': nrm(ks[0], (BATCH, SEQ, D_MODEL), 1.0),
        'mem': nrm(ks[1], (BATCH, N_MEM, D_MODEL), 1.0),
        'positions': positions,
        'norm_mix_g': gain(ks[3], (L, D_MODEL)),
        'w_in': nrm(ks[4], (L, D_MODEL, IN_COLS), D_MODEL ** -0.5),
        'w_out': nrm(ks[5], (L, MIX_WIDTH, D_MODEL), MIX_WIDTH ** -0.5),
        'conv_b_w': nrm(ks[6], (L, CONV_B_WIDTH, B_WIDTH), CONV_B_WIDTH ** -0.5),
        'conv_b_b': nrm(ks[7], (L, B_WIDTH), 0.02),
        'ln_b_g': gain(ks[8], (L, B_WIDTH)),
        'ln_b_b': nrm(ks[9], (L, B_WIDTH), 0.02),
        'norm_cross_g': gain(ks[10], (L, D_MODEL)),
        'norm_mem_g': gain(ks[11], (L, D_MODEL)),
        'w_q_cross': nrm(ks[12], (L, D_MODEL, D_MODEL), D_MODEL ** -0.5),
        'w_k_cross': nrm(ks[13], (L, D_MODEL, D_MODEL), D_MODEL ** -0.5),
        'w_v_cross': nrm(ks[14], (L, D_MODEL, D_MODEL), D_MODEL ** -0.5),
        'w_o_cross': nrm(ks[15], (L, D_MODEL, D_MODEL), D_MODEL ** -0.5),
        'norm_ffn_g': gain(ks[16], (L, D_MODEL)),
        'w_gate': nrm(ks[17], (L, D_MODEL, D_FF), D_MODEL ** -0.5),
        'w_up': nrm(ks[18], (L, D_MODEL, D_FF), D_MODEL ** -0.5),
        'ffn_conv_w': nrm(ks[19], (L, FFN_CONV_WIDTH, D_FF), FFN_CONV_WIDTH ** -0.5),
        'ffn_conv_b': nrm(ks[20], (L, D_FF), 0.02),
        'w_down': nrm(ks[21], (L, D_FF, D_MODEL), D_FF ** -0.5),
        'norm_final_g': gain(ks[22], (D_MODEL,)),
    }

def second_block(x, mem, positions, norm_mix_g, w_in, w_out, conv_b_w, conv_b_b, ln_b_g, ln_b_b,
              norm_cross_g, norm_mem_g, w_q_cross, w_k_cross, w_v_cross, w_o_cross,
              norm_ffn_g, w_gate, w_up, ffn_conv_w, ffn_conv_b, w_down, norm_final_g):
    cos, sin = rope_tables(positions)
    for l in range(DEPTH):
        x = hybrid_layer(x, mem, cos, sin, norm_mix_g[l], w_in[l], w_out[l], conv_b_w[l], conv_b_b[l],
                         ln_b_g[l], ln_b_b[l], norm_cross_g[l], norm_mem_g[l], w_q_cross[l], w_k_cross[l],
                         w_v_cross[l], w_o_cross[l], norm_ffn_g[l], w_gate[l], w_up[l], ffn_conv_w[l],
                         ffn_conv_b[l], w_down[l])
    return rmsnorm(x, norm_final_g)


def setup_inputs(seed=0):
    out = dict(first_inputs(seed))
    for name, value in second_inputs(seed + 1).items():
        if name != "x":
            out[name + "_2"] = value
    return out


def reference(
    x, mem, positions, norm_g, mem_norm_g, w_in, mu_rkv, mu_wa, w0, w2, a0, a2, k_k, k_a, r_k,
    lnx_g, lnx_b, q_norm_g, k_norm_g, sinks, xq_norm_g, xk_norm_g, w_mem_kv, w_proj_a, w_proj_b,
    w_proj_c, w_out, mem_2, positions_2, norm_mix_g_2, w_in_2, w_out_2, conv_b_w_2, conv_b_b_2,
    ln_b_g_2, ln_b_b_2, norm_cross_g_2, norm_mem_g_2, w_q_cross_2, w_k_cross_2, w_v_cross_2,
    w_o_cross_2, norm_ffn_g_2, w_gate_2, w_up_2, ffn_conv_w_2, ffn_conv_b_2, w_down_2,
    norm_final_g_2,
):
    x = first_block(
        x, mem, positions, norm_g, mem_norm_g, w_in, mu_rkv, mu_wa, w0, w2, a0, a2, k_k, k_a,
        r_k, lnx_g, lnx_b, q_norm_g, k_norm_g, sinks, xq_norm_g, xk_norm_g, w_mem_kv, w_proj_a,
        w_proj_b, w_proj_c, w_out,
    )
    return second_block(
        x, mem_2, positions_2, norm_mix_g_2, w_in_2, w_out_2, conv_b_w_2, conv_b_b_2, ln_b_g_2,
        ln_b_b_2, norm_cross_g_2, norm_mem_g_2, w_q_cross_2, w_k_cross_2, w_v_cross_2,
        w_o_cross_2, norm_ffn_g_2, w_gate_2, w_up_2, ffn_conv_w_2, ffn_conv_b_2, w_down_2,
        norm_final_g_2,
    )


_drawn_inputs = setup_inputs


def setup_inputs(seed=0):
    import zlib

    import numpy as np

    out = dict(_drawn_inputs(seed))
    spreads = {}
    factors = {'mem_norm_g': 8.0,
     'w2': 3.443,
     'a0': 2.819,
     'k_k': 3.345,
     'lnx_g': 2.698,
     'lnx_b': 8.0,
     'q_norm_g': 8.0,
     'k_norm_g': 8.0,
     'sinks': 8.0,
     'xq_norm_g': 8.0,
     'xk_norm_g': 8.0,
     'norm_mix_g_2': 3.431,
     'conv_b_b_2': 3.574,
     'ln_b_g_2': 5.698,
     'ln_b_b_2': 7.142,
     'norm_cross_g_2': 8.0,
     'norm_mem_g_2': 8.0,
     'norm_ffn_g_2': 3.988,
     'ffn_conv_b_2': 6.032,
     'norm_final_g_2': 2.952}
    for name, (base, spread) in spreads.items():
        noise = np.random.default_rng([zlib.crc32(name.encode()), seed]).standard_normal(out[name].shape)
        drawn = base * np.exp(spread * noise) if base else spread * noise
        out[name] = __import__('jax').numpy.asarray(drawn.astype(out[name].dtype))
    for name, factor in factors.items():
        out[name] = (out[name] * factor).astype(out[name].dtype)
    return out
```

```python
import math
from contextlib import ExitStack

import numpy as np
import concourse.bass as bass
from concourse import mybir

P = 128
T = 512
NT = T // P
D = 1024
KD = D // P
M = 256
HD = 64
C = 64
RW = 4
FF = 2816 // P
TAPS, FTAPS = 31, 3
TOPK = min(256, T // 4)
SEL = NT - 1
RING = 4
PB = 8
MASKED = -1e30
TAKEN = -3.3e38
EXP_HALF = math.exp(-0.5)
LN_SHIFT = 30
TWO_PI = (6.28125, 1014.0 / 2 ** 19, 2 * math.pi - 6.28125 - 1014.0 / 2 ** 19)
ROUND = 1.5 * 2 ** 23

COLS = {}
for _name, _n in (("norm_g", 8), ("mem_norm_g", 8), ("mu", 13), ("w0", 4), ("a0", 4), ("k_k", 4), ("k_a", 4),
                  ("r_k", 4), ("lnx_g", 4), ("lnx_b", 4), ("q_g", 1), ("k_g", 1), ("xq_g", 1), ("xk_g", 1),
                  ("sinks", 8), ("norm_mix_g", 8), ("norm_cross_g", 8), ("norm_mem_g", 8), ("norm_ffn_g", 8),
                  ("norm_final_g", 8), ("ln_b_g", 4), ("ln_b_b", 4), ("conv_w", 4 * TAPS), ("conv_b", 4),
                  ("ffn_w", FF * FTAPS), ("ffn_b", FF),
                  ("freq", 1), ("freq2", 1), ("eps6", 1), ("eps_lnx", 1), ("zero", 1), ("kk_eps", 1), ("kk_bias", 1),
                  ("half_pi", 1)):
    COLS[_name] = (sum(n for _, n in COLS.values()), _n)
NCOLS = sum(n for _, n in COLS.values())

CST = {}
for _name, _n in (("ones", P), ("head_ones", P), ("ident", P), ("ident64", HD), ("rot", P), ("dup0", P), ("dup1", P),
                  ("rotdup0", P), ("rotdup1", P), ("rot2", P), ("rot2dup0", P), ("rot2dup1", P),
                  ("level0", P), ("levelT", 6 * P), ("strictT", P), ("inclT", P), ("causal", 2 * P),
                  ("band", 2 * P), ("restart", T)):
    CST[_name] = (sum(n for _, n in CST.values()), _n)
NCST = sum(n for _, n in CST.values())


def constants():
    c = np.zeros((P, NCST), np.float32)

    def put(name, a):
        o, n = CST[name]
        c[:, o:o + n] = a.reshape(P, n)

    i = np.arange(P)
    row, col = i[:, None], i[None, :]
    put("ones", np.ones((P, P)))
    put("head_ones", (row // HD == col // HD) * 1.0)
    put("ident", np.eye(P))
    put("ident64", np.concatenate([np.eye(HD)] * 2))

    def rotation(half):
        r = np.zeros((P, P))
        for m in range(P):
            d = m % HD
            if d < half:
                r[m + half, m] = -1
            elif d < 2 * half:
                r[m - half, m] = 1
        return r

    dup = []
    for s in range(2):
        d = np.zeros((P, P))
        for m in range(P):
            d[s * HD + m % HD, m] = 1
        dup.append(d)
    put("rot", rotation(HD // 2))
    put("rot2", rotation(8))
    for s in range(2):
        put(f"dup{s}", dup[s])
        put(f"rotdup{s}", dup[s] @ rotation(HD // 2))
        put(f"rot2dup{s}", dup[s] @ rotation(8))
    levels = []
    for l in range(6):
        s = 1 << l
        levels.append((row // (2 * s) == col // (2 * s)) & ((row // s) % 2 == 1) & ((col // s) % 2 == 0))
    put("level0", levels[0] * 1.0)
    put("levelT", np.stack([m.T for m in levels], 1) * 1.0)
    put("strictT", ((row < col) & (row // C == col // C)) * 1.0)
    put("inclT", ((row <= col) & (row // C == col // C)) * 1.0)
    after = np.where(col > row, MASKED, 0.0)
    put("causal", np.concatenate([np.zeros((P, P)), after], 1))
    put("band", np.concatenate([np.where(col > row, 0.0, MASKED), after], 1))
    put("restart", np.broadcast_to((np.arange(T) % C != 0) * 1.0, (P, T)))
    return c


class Signal:

    def __init__(self, sem):
        self.sem, self.n = sem, 0

    def inc(self, ins):
        ins.then_inc(self.sem, 1)
        self.n += 1


def build(nc, xt, memt, mem2t, weights, cols_d, cst_d, wa2_d, pos_d, pos2_d, out_d):
    f32 = mybir.dt.float32
    i32 = mybir.dt.int32
    ALU = mybir.AluOpType
    ACT = mybir.ActivationFunctionType
    AX = mybir.AxisListType.X
    ADD, SUB, MUL, MAX, MIN = ALU.add, ALU.subtract, ALU.mult, ALU.max, ALU.min

    with ExitStack() as ctx:
        def sb(name, shape, dt=f32):
            return ctx.enter_context(nc.sbuf_tensor(name, shape, dt))

        def signal(name):
            return Signal(ctx.enter_context(nc.semaphore(name)))

        x = sb("x", [P, KD, T])
        h = sb("h", [P, KD, T])
        ring = sb("ring", [P, RING, PB, P])
        cst = sb("cst", [P, NCST])
        cols = sb("cols", [P, NCOLS])
        half = sb("half", [P, NCOLS])
        trig = sb("trig", [P, 2, T])
        sq = sb("sq", [P, 4, T])
        tmp = sb("tmp", [P, 4, T])
        small = sb("small", [P, 2, 16])
        ARENA = 31300
        arena = sb("arena", [P, ARENA])
        top = [0]

        def take(*shape):
            n = int(np.prod(shape))
            a = arena[:, top[0]:top[0] + n]
            top[0] += n
            assert top[0] <= ARENA, (top, shape)
            names = "abc"[:len(shape)]
            if len(shape) == 1:
                return a
            return a.rearrange(f"p ({' '.join(names)}) -> p {' '.join(names)}",
                               **{m: s for m, s in zip(names[1:], shape[1:])})

        ya, yb, yc = take(4, T), take(4, T), take(4, T)
        r, k, v = take(4, T), take(4, T), take(4, T)
        kk, bb = take(4, T), take(4, T)
        bonus = take(4, T)
        mem = take(KD, M)
        memq = mem.rearrange("p a b -> p (a b)").rearrange("p (a b) -> p a b", a=4)
        arena2 = top[0]
        wa2 = bonus[:, 3, :]
        xq, km, vm = take(4, T), take(4, M), take(2, T)
        skd, sv = take(2, T), take(NT, P)
        S, Pr, PT = take(2, T), take(2, T), take(2, T)
        raw = take(2, 514)
        lwa, skn = skd[:, 0, :], skd[:, 1, :]
        thz = take(2, T)
        E = [S[:, 0], S[:, 1], Pr[:, 0], Pr[:, 1], PT[:, 0], PT[:, 1]]
        gexp = sb("gexp", [P, 4, 8])
        end_attn = top[0]
        top[0] = arena2
        bT, kT, vT = take(T), take(T), take(T)
        aT = take(8, P)
        AB, AK, RB, RK = take(T), take(T), take(T), take(T)
        XX, XT, YT = take(T), take(T), take(T)
        ML = take(2, T)
        WU = take(4, P)
        MT, NN = take(2, 4 * HD), take(2, 4 * HD)
        St = take(2, 4 * HD)
        top[0] = max(top[0], end_attn)
        rwy = memq
        merged = arena[:, 3 * 2048:5 * 2048].rearrange("p (a b) -> p a b", a=8)
        gt = arena[:, 5 * 2048:5 * 2048 + 6 * T].rearrange("p (a b) -> p a b", a=6)
        top[0] = 0
        mem2 = take(KD, M)
        k2, v2 = take(KD, M), take(2, D)
        mix = take(8, T)
        q2, qi, kd, kid = take(4, T), take(2, T), take(T), take(T)
        vwi = take(NT, 68)
        sc, sel = take(SEL, T), take(SEL, T)
        rel = take(2, T)
        u = take(4, TAPS - 1 + T)
        thg, ga = take(2, T), take(2, T)
        kraw = take(T)
        S2, P2, PT2 = take(2, T), take(2, T), take(2, T)
        max8 = sb("max8", [P, SEL, 8])
        sq_hi2 = take(4, T)
        top[0] = 3 * 2048
        qc, oc = take(8, T), take(8, T)
        top[0] = 0
        prod = take(FF, T)
        gpad = take(2, T + FTAPS - 1)
        upr, cv, thf = take(2, T), take(2, T), take(2, T)

        bank = [ctx.enter_context(nc.psum_tensor(f"bank{i}", [P, T], f32)) for i in range(8)]

        def col(name, i=0, n=1, of=cols):
            o, m = COLS[name]
            assert i + n <= m
            return of[:, o + i:o + i + n]

        def con(name, i=0, n=P):
            o, m = CST[name]
            return cst[:, o + i * n:o + (i + 1) * n]

        def tok(t, n=P):
            return slice(t * n, (t + 1) * n)

        panel_in = [signal(f"panel_in{s}") for s in range(RING)]
        x_in = [signal(f"x_in{i}") for i in range(4)]
        cst_in, cols_in, wa2_in, pos_in, pos2_in, mem_in, mem2_in, out_done = (signal(n) for n in (
            "cst_in", "cols_in", "wa2_in", "pos_in", "pos2_in", "mem_in", "mem2_in", "out_done"))
        dense_done = signal("dense_done")
        dense_act, dense_dve = signal("dense_read_by_act"), signal("dense_read_by_dve")
        v_done, v_read = signal("vbank_done"), signal("vbank_read")
        a_done, a_read = signal("abank_done"), signal("abank_read")
        o_done, o_read = signal("obank_done"), signal("obank_read")
        act_chain, dve_chain, pool_chain = signal("act_chain"), signal("dve_chain"), signal("pool_chain")
        halves, trig_ready = signal("halves"), signal("trig_ready")
        sq_ready, rinv_ready, norm_applied = signal("sq_ready"), signal("rinv_ready"), signal("norm_applied")
        raw_ready, raw_used = signal("raw_ready"), signal("raw_used")
        lora_ready, decay_ready, exps_ready, head_done, rk_ready = (signal(n) for n in (
            "lora_ready", "decay_ready", "exps_ready", "head_done", "rk_ready"))
        th_ready, silu_done = signal("th_ready"), signal("silu_done")
        rope_in, rope_done = signal("rope_in"), signal("rope_done")
        bias_ready, exp_done, p_ready, pt_ready = (signal(n) for n in ("bias_ready", "exp_done", "p_ready", "pt_ready"))
        tm_ready, gram_ready, ml_ready, ml_free, wu_ready, state_ready, y_ready = (signal(n) for n in (
            "tm_ready", "gram_ready", "ml_ready", "ml_free", "wu_ready", "state_ready", "y_ready"))
        inv_ready, mn_ready, av_ready = signal("inv_ready"), signal("mn_ready"), signal("av_ready")
        lnx_ready = signal("lnx_ready")
        merged_ready, gate_used = signal("merged_ready"), signal("gate_used")
        block1_done, glu_ready, glu_used, u_ready = (signal(n) for n in ("block1_done", "glu_ready", "glu_used", "u_ready"))
        rel_ready, rel_used = signal("rel_ready"), signal("rel_used")
        conv_ready, mix_ready, conv_th = signal("conv_ready"), signal("mix_ready"), signal("conv_th")
        ffn_g, ffn_c, ffn_th, ffn_prod = (signal(n) for n in ("ffn_g", "ffn_c", "ffn_th", "ffn_prod"))
        x_final = signal("x_final")
        sin_ready, decay_th, u_zero = (signal(n) for n in ("sin_ready", "decay_th", "u_zero"))
        pe_rows = signal("pe_rows")

        groups = []
        for n in range(13):
            groups.append(("act", 8))
        for n in range(8):
            groups.append(("act", 8))
        for n in range(22):
            groups.append(("act", 8))
        for n in range(8):
            groups += [("act", 8)] * 3 + [("proj", 4)] * 3
        groups += [("dve", 8)] * 8
        groups += [("act", 8)] * 16
        groups += [("act", 8)] * 16
        groups += [("dve", 8)] * 8
        groups += [("act", 8)] * 8
        groups += [("dve", 8)] * 8
        groups += [("act", 8)] * (2 * FF)
        groups += [("dve", FF)] * 8
        nblocks = sum(n for _, n in groups)
        uses, n_use = {}, 0
        for g, (who, _) in enumerate(groups):
            if who != "proj":
                uses[g] = n_use
                n_use += 1
        DQ = 13 + 8 + 22 + 24
        DC = DQ + 16 + 16
        DF = DC + 8
        assert nblocks == weights.shape[0] * PB, (nblocks, weights.shape)
        NPANEL = nblocks // PB
        last_user = []
        nb = 0
        for g, (_, n) in enumerate(groups):
            nb += n
            while len(last_user) < nb // PB:
                last_user.append(g + 1)

        def window_jobs():
            jobs = []
            for b in range(NT):
                for pair in range(4):
                    kv = pair // 2
                    k0 = max(b - 1, 0) * P
                    nk = (b + 1) * P - k0
                    score = [[(memq[64 * u_:64 * u_ + 64, pair, tok(b)], skd[64 * u_:64 * u_ + 64, kv, k0:k0 + nk])]
                             for u_ in range(2)]
                    pv = [(lambda o, u_=u_: o[64 * u_:64 * u_ + 64, 0:P],
                           [(sv[:, k0 // P + s, kv * HD:kv * HD + HD], lambda pt, s=s, u_=u_: pt[:, (2 * s + u_) * P:(2 * s + u_ + 1) * P])
                            for s in range(nk // P)]) for u_ in range(2)]
                    mask = con("causal", 1) if b == 0 else con("band", 0, 2 * P)
                    jobs.append((nk, HD ** -0.5, score, mask, col("sinks", 2 * pair, 2), pv,
                                 lambda o: o[:, 0:P], yb[:, pair, tok(b)], yb[:, pair, tok(b)]))
            return jobs

        def memory_jobs():
            jobs = []
            for hd in range(4):
                for j in range(2):
                    score = [[(xq[:, hd, tok(2 * j + u_)], km[:, hd, :])] for u_ in range(2)]
                    pv = [(lambda o: o[:, 0:2 * P],
                           [(vm[:, s, tok(hd)], lambda pt, s=s: pt[:, 2 * s * P:2 * (s + 1) * P]) for s in range(2)])]
                    dst = yc[:, hd, tok(j, 2 * P)]
                    jobs.append((M, P ** -0.5, score, None, None, pv, lambda o: o[:, 0:2 * P], dst, dst))
            return jobs

        def sparse_jobs():
            jobs = []
            for b in range(NT):
                nk = (b + 1) * P
                mask = con("causal", 1) if b == 0 else sel[:, b - 1, 0:nk]
                for pair in range(4):
                    for us in ([0, 1],) if b < 2 else ([0], [1]):
                        score = [[(q2[64 * u_:64 * u_ + 64, pair, tok(b)], kd[64 * u_:64 * u_ + 64, 0:nk])] for u_ in us]
                        n = len(us)
                        pv = [(lambda o, u_=u_: o[64 * u_:64 * u_ + 64, 0:P],
                               [(vwi[:, s, 0:HD], lambda pt, s=s, i=i, n=n: pt[:, (n * s + i) * P:(n * s + i + 1) * P])
                                for s in range(nk // P)]) for i, u_ in enumerate(us)]
                        lo, hi = 64 * us[0], 64 * us[-1] + 64
                        jobs.append((nk, HD ** -0.5, score, mask, None, pv, lambda o, lo=lo, hi=hi: o[lo:hi, 0:P],
                                     mix[lo:hi, pair, tok(b)], None))
            return jobs

        def cross_jobs():
            jobs = []
            for hd in range(4):
                for j in range(2):
                    score = [[(qc[:, 2 * hd + c, tok(2 * j + u_)], k2[:, 2 * hd + c, :]) for c in range(2)] for u_ in range(2)]
                    pv = [(lambda o, c=c: o[:, 2 * c * P:2 * (c + 1) * P],
                           [(v2[:, s, tok(2 * hd + c)], lambda pt, s=s: pt[:, 2 * s * P:2 * (s + 1) * P]) for s in range(2)])
                          for c in range(2)]
                    jobs.append((M, (2 * P) ** -0.5, score, None, None, pv,
                                 lambda o: o[:, :].rearrange("p (c t) -> p c t", c=2),
                                 oc[:, 2 * hd:2 * hd + 2, tok(j, 2 * P)], None))
            return jobs

        block = ctx.enter_context(nc.Block())

        @block.tensor
        def _(pe):
            mm = nc.tensor.matmul
            bufs = {"att": (S, Pr, PT), "sq": kk}

            def slot(i):
                return sq[:, i, :] if i < 4 else bufs["sq"][:, i - 4, :]

            def mean_square(i):
                return bufs["att"][i // 2][:, i % 2, :]

            state = {"block": 0, "group": 0, "v": 0, "a": 0, "o": 0, "sq": 0}
            reads = {"act": 0, "dve": 0}
            dense_banks = []

            def weight():
                b = state["block"]
                state["block"] += 1
                p = b // PB
                if b % PB == 0:
                    pe.wait_ge(panel_in[p % RING].sem, 16 * (p // RING + 1))
                return ring[:, p % RING, b % PB, :]

            def dense_bank():
                who = groups[state["group"]][0]
                n = len(dense_banks)
                if n >= 2:
                    w, c = dense_banks[n - 2]
                    pe.wait_ge((dense_act if w == "act" else dense_dve).sem, c)
                reads[who] += 1
                dense_banks.append((who, reads[who]))
                return bank[n % 2]

            def end_group(last):
                dense_done.inc(last)
                state["group"] += 1

            def dense(src, kt=KD, n=T):
                o = dense_bank()
                for c in range(kt):
                    last = mm(o[:, 0:n], weight(), src[:, c, :], start=c == 0, stop=c == kt - 1)
                end_group(last)

            def dense_tokens(src, tiles, n=P):
                o = dense_bank()
                w = [weight() for _ in range(KD)]
                for t in range(tiles):
                    for c in range(KD):
                        last = mm(o[:, t * n:(t + 1) * n], src[:, c, tok(t)], w[c][:, 0:n], start=c == 0, stop=c == KD - 1)
                end_group(last)

            def other_rows(last):
                pe_rows.inc(last)
                pe.wait_ge(pe_rows.sem, pe_rows.n)

            rings = {"v": (2, v_done, v_read), "a": (4, a_done, a_read), "o": (6, o_done, o_read)}

            def take_bank(kind):
                b0, done, read = rings[kind]
                n = state[kind]
                state[kind] += 1
                if n >= 2:
                    pe.wait_ge(read.sem, n - 1)
                return bank[b0 + n % 2]

            def norm_sums(ones, norms, tiles, n=T):
                for i in range(norms):
                    o = take_bank("a")
                    for c in range(tiles):
                        state["sq"] += 1
                        pe.wait_ge(sq_ready.sem, state["sq"])
                        s = slot(i * tiles + c)
                        last = mm(o[:, 0:n], ones, s[:, 0:n], start=c == 0, stop=c == tiles - 1)
                    a_done.inc(last)

            def single(kind, lhsT, rhs, n=T):
                o = take_bank(kind)
                rings[kind][1].inc(mm(o[:, 0:n], lhsT, rhs, start=True, stop=True))

            att = {"p": 0, "pt": 0}

            def attention(jobs):
                n = len(jobs)
                for i in range(n + 2):
                    if i < n:
                        nk, _, score, *_ = jobs[i]
                        o = take_bank("v")
                        for u_, parts in enumerate(score):
                            if u_ and parts[0][0].base_partition() != score[0][0][0].base_partition():
                                other_rows(last)
                            for c, (a, b) in enumerate(parts):
                                last = mm(o[:, u_ * nk:(u_ + 1) * nk], a, b, start=c == 0, stop=c == len(parts) - 1)
                        v_done.inc(last)
                    if 1 <= i <= n:
                        nk, _, score, *_ = jobs[i - 1]
                        U = len(score)
                        att["p"] += 1
                        pe.wait_ge(p_ready.sem, att["p"])
                        o = take_bank("a")
                        pbuf = bufs["att"][1][:, (att["p"] - 1) % 2]
                        for s in range(nk // P):
                            for u_ in range(U):
                                last = nc.tensor.transpose(o[:, (U * s + u_) * P:(U * s + u_ + 1) * P],
                                                           pbuf[:, u_ * nk + s * P:u_ * nk + (s + 1) * P], con("ident"))
                        a_done.inc(last)
                    if i >= 2:
                        pv = jobs[i - 2][5]
                        att["pt"] += 1
                        pe.wait_ge(pt_ready.sem, att["pt"])
                        o = take_bank("o")
                        pt = bufs["att"][2][:, (att["pt"] - 1) % 2]
                        for view, parts in pv:
                            for s, (vs, ps) in enumerate(parts):
                                last = mm(view(o), vs, ps(pt), start=s == 0, stop=s == len(parts) - 1)
                        o_done.inc(last)

            pe.wait_ge(cst_in.sem, 16)
            norm_sums(con("ones"), 1, KD)
            norm_sums(con("ones"), 1, KD, M)
            pe.wait_ge(norm_applied.sem, 1)
            for n in range(13):
                dense(h)
            pe.wait_ge(norm_applied.sem, 2)
            for n in range(4):
                dense(mem, n=M)
            for n in range(4):
                dense_tokens(mem, 2)
            norm_sums(con("head_ones"), 4, 1)
            pe.wait_ge(wa2_in.sem, 16)
            pe.wait_ge(lora_ready.sem, 1)
            plan = [6, 6, 5, 5]
            n = 13
            for i in range(4):
                single("a", wa2[0:64, tok(i)], lwa[0:64, :])
                single("a", wa2[64:128, tok(i)], lwa[64:128, :])
                for _ in range(plan[i]):
                    if n == 22:
                        dense_tokens(h, NT)
                    else:
                        dense(h)
                    n += 1
                pe.wait_ge(rk_ready.sem, i + 1)
                single("v", con("head_ones"), E[0])

            norm_sums(con("head_ones"), 4, 1)
            norm_sums(con("head_ones"), 1, 1)
            for i in range(4):
                pe.wait_ge(rope_in.sem, i + 1)
                single("v", con("rot"), memq[:, i, :])
            pe.wait_ge(rope_in.sem, 5)
            for s in range(2):
                single("v", con(f"dup{s}"), skn)
                single("v", con(f"rotdup{s}"), skn)
            norm_sums(con("ones"), 4, 1)
            norm_sums(con("ones"), 4, 1, M)
            pe.wait_ge(rope_done.sem, 6)
            pe.wait_ge(norm_applied.sem, 2 + 4 + 5 + 8)
            attention(window_jobs() + memory_jobs())

            n_gram = n_ml = n_inv = n_av = n_wu = n_mn = 0
            for t in range(NT):
                for src in (bb, kk, k, v):
                    pe.wait_ge(head_done.sem, 4)
                    o = take_bank("a")
                    for i in range(4):
                        last = nc.tensor.transpose(o[:, tok(i)], src[:, i, tok(t)], con("ident"))
                    a_done.inc(last)
                for hb in range(2):
                    heads = [(4 * hb + j, (4 * hb + j) // 2, 64 * (j % 2)) for j in range(4)]
                    for lhs, rhs in ((kk, bb), (bb, kk), (k, kk), (bb, r), (k, r)):
                        o = take_bank("v")
                        for j in (0, 2, 1, 3):
                            hd, i, p0 = heads[j]
                            if j == 1:
                                other_rows(last)
                            last = mm(o[:, tok(j)], lhs[p0:p0 + 64, i, tok(t)], rhs[p0:p0 + 64, i, tok(t)], start=True, stop=True)
                        v_done.inc(last)
                    n_gram += 3
                    pe.wait_ge(gram_ready.sem, n_gram - 1)
                    pe.wait_ge(tm_ready.sem, 4 * (t + 1))
                    o = take_bank("a")
                    for j, (hd, i, p0) in enumerate(heads):
                        last = mm(o[:, j * HD:(j + 1) * HD], AK[:, tok(j)], vT[:, tok(hd, HD)], start=True, stop=True)
                    a_done.inc(last)
                    for l in range(1, 6):
                        n_ml += 1
                        pe.wait_ge(ml_ready.sem, n_ml)
                        if l > 1:
                            pe.wait_ge(inv_ready.sem, n_inv)
                        o = take_bank("a")
                        for j in range(4):
                            last = mm(o[:, tok(j)], ML[:, n_ml % 2, tok(j)], XX[:, tok(j)], start=True, stop=True)
                        a_done.inc(last)
                        pe.wait_ge(y_ready.sem, n_ml)
                        if l < 5:
                            o = take_bank("v")
                            for j in range(4):
                                last = mm(o[:, tok(j)], XT[:, tok(j)], YT[:, tok(j)], start=True, stop=True)
                            v_done.inc(last)
                        o = take_bank("v")
                        for j in range(4):
                            last = mm(o[:, tok(j)], YT[:, tok(j)], XT[:, tok(j)], start=True, stop=True)
                        v_done.inc(last)
                        n_inv += 1
                    pe.wait_ge(inv_ready.sem, n_inv)
                    n_av += 1
                    pe.wait_ge(av_ready.sem, n_av)
                    o = take_bank("a")
                    for j, (hd, i, p0) in enumerate(heads):
                        last = mm(o[:, tok(j)], XT[:, tok(j)], aT[:, hd, :], start=True, stop=True)
                    a_done.inc(last)
                    n_wu += 1
                    pe.wait_ge(wu_ready.sem, n_wu)
                    pe.wait_ge(gram_ready.sem, 3 * n_wu)
                    o = take_bank("v")
                    for j, (hd, i, p0) in enumerate(heads):
                        last = mm(o[p0:p0 + 64, (j // 2) * P:(j // 2 + 1) * P], WU[:, j, 0:HD], RB[:, tok(j)], start=True, stop=True)
                    v_done.inc(last)
                    o = take_bank("v")
                    for j, (hd, i, p0) in enumerate(heads):
                        ov = o[p0:p0 + 64, (j // 2) * P:(j // 2 + 1) * P]
                        mm(ov, WU[:, j, HD:P], RB[:, tok(j)], start=True, stop=False)
                        last = mm(ov, vT[:, tok(hd, HD)], RK[:, tok(j)], start=False, stop=True)
                    v_done.inc(last)
                    o = take_bank("v")
                    for c in range(2):
                        cr = slice(64 * c, 64 * c + 64)
                        if c:
                            other_rows(last)
                        for j, (hd, i, p0) in enumerate(heads):
                            q0 = (c * 2 + j // 2) * HD
                            last = mm(o[p0:p0 + 64, q0:q0 + HD], WU[cr, j, 0:HD], bT[cr, tok(hd, HD)], start=True, stop=True)
                    v_done.inc(last)
                    o = take_bank("v")
                    for c in range(2):
                        cr = slice(64 * c, 64 * c + 64)
                        if c:
                            other_rows(last)
                        for j, (hd, i, p0) in enumerate(heads):
                            q0 = (c * 2 + j // 2) * HD
                            mm(o[p0:p0 + 64, q0:q0 + HD], bT[cr, tok(hd, HD)], WU[cr, j, HD:P], start=True, stop=False)
                            last = mm(o[p0:p0 + 64, q0:q0 + HD], kT[cr, tok(hd, HD)], vT[cr, tok(hd, HD)], start=False, stop=True)
                    v_done.inc(last)
                pe.wait_ge(mn_ready.sem, 2 * (t + 1))
                for c in range(2):
                    cc = 2 * t + c
                    if cc == 0:
                        continue
                    pe.wait_ge(state_ready.sem, cc)
                    s = St[:, cc % 2]
                    o = take_bank("v")
                    for hd in range(8):
                        i, p0 = hd // 2, 64 * (hd % 2)
                        last = mm(o[p0:p0 + 64, i * C:(i + 1) * C], s[p0:p0 + 64, i * HD:(i + 1) * HD],
                                  r[p0:p0 + 64, i, tok(cc, C)], start=True, stop=True)
                    v_done.inc(last)
                    if cc < 7:
                        o = take_bank("v")
                        for hd in range(8):
                            i, p0 = hd // 2, 64 * (hd % 2)
                            last = mm(o[p0:p0 + 64, i * HD:(i + 1) * HD], MT[p0:p0 + 64, c, i * HD:(i + 1) * HD],
                                      s[p0:p0 + 64, i * HD:(i + 1) * HD], start=True, stop=True)
                        v_done.inc(last)
            for i in range(4):
                pe.wait_ge(lnx_ready.sem, 1)
                single("v", con("head_ones"), rwy[:, i, :])
            norm_sums(con("head_ones"), 4, 1)
            for j in range(8):
                for g in range(3):
                    dense(h)
                if j == 0:
                    pe.wait_ge(norm_applied.sem, 2 + 4 + 5 + 8 + 4)
                for y in (ya, yb, yc):
                    o = take_bank("v")
                    for c in range(4):
                        last = mm(o[:, :], weight(), y[:, c, :], start=c == 0, stop=c == 3)
                    end_group(last)
            pe.wait_ge(merged_ready.sem, 8)
            for j in range(8):
                dense(merged)

            bufs.update(att=(S2, P2, PT2), sq=sq_hi2)
            norm_sums(con("ones"), 1, KD)
            norm_sums(con("ones"), 1, KD, M)
            NA = 2 + 4 + 5 + 8 + 4
            pe.wait_ge(norm_applied.sem, NA + 1)
            for n in range(7):
                dense(h)
            dense_tokens(h, NT, 68)
            for n in range(8):
                dense(h)
            pe.wait_ge(norm_applied.sem, NA + 2)
            for i in range(4):
                pe.wait_ge(dense_act.sem, DQ + i + 1)
                single("v", con("rot2"), q2[:, i, :])
            for i in range(2):
                pe.wait_ge(dense_act.sem, DQ + 7)
                single("v", con("rot2"), qi[:, i, :])
            for s in range(2):
                single("v", con(f"dup{s}"), kraw)
                single("v", con(f"rot2dup{s}"), kraw)
            pe.wait_ge(rope_done.sem, 6 + 8)
            for t in range(SEL):
                nk = (2 + t) * P
                for hd in range(4):
                    p0 = 64 * (hd % 2)
                    single("a", qi[p0:p0 + 64, hd // 2, tok(1 + t)], kid[p0:p0 + 64, 0:nk], nk)
            for n in range(8):
                dense(mem2, n=M)
            for n in range(8):
                dense_tokens(mem2, 2)
            attention(sparse_jobs())
            for i in range(4):
                pe.wait_ge(conv_ready.sem, 4)
            o = take_bank("v")
            for i in range(4):
                last = mm(o[:, :], con("ones"), mix[:, 4 + i, :], start=i == 0, stop=i == 3)
            v_done.inc(last)
            norm_sums(con("ones"), 1, 4)
            pe.wait_ge(mix_ready.sem, 4)
            for j in range(8):
                dense(mix)
            norm_sums(con("ones"), 1, KD)
            pe.wait_ge(norm_applied.sem, NA + 4)
            for j in range(8):
                dense(h)
            pe.wait_ge(dense_act.sem, DC + 8)
            attention(cross_jobs())
            pe.wait_ge(o_read.sem, state["o"])
            for j in range(8):
                dense(oc)
            norm_sums(con("ones"), 1, KD)
            pe.wait_ge(norm_applied.sem, NA + 5)
            for f in range(FF):
                dense(h)
                dense(h)
            pe.wait_ge(ffn_prod.sem, FF)
            for j in range(8):
                dense(prod, FF)
            norm_sums(con("ones"), 1, KD)
            assert state["group"] == len(groups) and state["block"] == nblocks

        @block.scalar
        def _(act):
            fn = nc.scalar.activation
            bufs = {"att": (S, Pr, PT), "sq": kk}

            def slot(i):
                return sq[:, i, :] if i < 4 else bufs["sq"][:, i - 4, :]

            def mean_square(i):
                return bufs["att"][i // 2][:, i % 2, :]

            st = {"dense": 0, "a": 0, "norm": 0, "th": 0, "p": 0, "pt": 0}
            dense_ids = [g for g, (w, _) in enumerate(groups) if w == "act"]

            def do(ins, sig=act_chain):
                sig.inc(ins)
                act.wait_ge(sig.sem, sig.n)

            def dense_in():
                g = dense_ids[st["dense"]]
                act.wait_ge(dense_done.sem, g + 1)
                st["dense"] += 1
                return bank[uses[g] % 2]

            def a_in():
                st["a"] += 1
                act.wait_ge(a_done.sem, st["a"])
                return bank[4 + (st["a"] - 1) % 2]

            def norms(srcs, tiles, ln_scale, eps, out_bias="zero", n=T, scales=None, refined=False):
                act.wait_ge(norm_applied.sem, st["norm"])
                for i, s in enumerate(srcs):
                    do(fn(slot(i)[:, 0:n], s, ACT.Square, scale=1.0 if scales is None else scales[i]), sq_ready)
                cnt = len(srcs) // tiles
                for i in range(cnt):
                    o = a_in()
                    if refined:
                        do(fn(mean_square(i)[:, 0:n], o[:, 0:n], ACT.Identity, bias=eps, scale=ln_scale))
                    do(fn(sq[:, i, 0:n], o[:, 0:n], ACT.Ln, bias=eps, scale=ln_scale), a_read)
                for i in range(cnt):
                    do(fn(sq[:, i, 0:n], sq[:, i, 0:n], ACT.Exp, bias=col(out_bias), scale=-0.5), rinv_ready)
                st["norm"] += cnt

            def silu_in(dst):
                o = dense_in()
                n = st["th"]
                if n >= 2:
                    act.wait_ge(silu_done.sem, n - 1)
                do(fn(dst, o[:, :], ACT.Copy, scale=0.5))
                do(fn(thz[:, n % 2], o[:, :], ACT.Tanh, scale=0.5), th_ready)
                dense_act_inc()
                st["th"] += 1

            def dense_act_inc():
                act.sem_inc(dense_act.sem, 1)
                dense_act.n += 1

            def copy_dense(dst, src, **kw):
                do(fn(dst, src, ACT.Copy, **kw), dense_act)

            def attention(jobs):
                n = len(jobs)
                for i in range(n + 1):
                    if i < n:
                        nk, scale, score, mask, sinks, *_ = jobs[i]
                        st["p"] += 1
                        act.wait_ge(bias_ready.sem, st["p"])
                        s = (st["p"] - 1) % 2
                        sbuf, pbuf, _ = bufs["att"]
                        for u_ in range(len(score)):
                            if sinks is not None:
                                do(fn(small[:, s, 6 + u_:7 + u_], sinks[:, u_:u_ + 1], ACT.Exp, bias=small[:, s, 2 + u_:3 + u_], scale=1.0))
                            do(fn(pbuf[:, s, u_ * nk:(u_ + 1) * nk], sbuf[:, s, u_ * nk:(u_ + 1) * nk], ACT.Exp,
                                  bias=small[:, s, 2 + u_:3 + u_], scale=scale, accum_out=small[:, s, 4 + u_:5 + u_]),
                               exp_done if u_ == len(score) - 1 else act_chain)
                    if i >= 1:
                        nk, _, score, *_ = jobs[i - 1]
                        o = a_in()
                        st["pt"] += 1
                        if st["pt"] > 2:
                            act.wait_ge(o_done.sem, st["pt"] - 2)
                        w = len(score) * nk
                        do(fn(bufs["att"][2][:, (st["pt"] - 1) % 2, 0:w], o[:, 0:w], ACT.Copy), pt_ready)
                        a_read_inc()

            def a_read_inc():
                act.sem_inc(a_read.sem, 1)
                a_read.n += 1

            act.dma_start(cst[:, :], cst_d).then_inc(cst_in.sem, 16)
            act.dma_start(cols[:, :], cols_d).then_inc(cols_in.sem, 16)
            act.dma_start(tmp[:, 0].bitcast(i32), pos_d).then_inc(pos_in.sem, 16)
            act.dma_start(mem, memt).then_inc(mem_in.sem, 16)
            act.dma_start(wa2, wa2_d).then_inc(wa2_in.sem, 16)
            act.wait_ge(cols_in.sem, 16)
            for i in range(4):
                act.wait_ge(x_in[i].sem, 16)
            norms([x[:, i, :] for i in range(KD)], KD, 1.0 / D, col("eps6"))
            act.wait_ge(mem_in.sem, 16)
            norms([mem[:, i, :] for i in range(KD)], KD, 1.0 / D, col("eps6"), n=M)
            act.wait_ge(trig_ready.sem, 1)
            do(fn(trig[:, :, :], trig[:, :, :], ACT.Sin), sin_ready)
            act.wait_ge(raw_used.sem, 1)
            for n in range(13):
                o = dense_in()
                if n >= 2:
                    act.wait_ge(raw_used.sem, n)
                do(fn(raw[:, n % 2, 1:T + 1], o[:, :], ACT.Copy), raw_ready)
                dense_act_inc()
            for n in range(4):
                copy_dense(km[:, n, :], dense_in()[:, 0:M])
            for n in range(4):
                copy_dense(vm[:, :, tok(n)], dense_in()[:, 0:M].rearrange("p (s d) -> p s d", s=2))
            act.wait_ge(raw_used.sem, 1 + 13)
            norms([k[:, i, :] for i in range(4)], 1, 2.0 ** LN_SHIFT, col("kk_eps"), "kk_bias", scales=[col("k_k", i) for i in range(4)])
            do(fn(lwa[0:64, :], lwa[0:64, :], ACT.Tanh), lora_ready)
            dense_dst = ([lambda n=n: silu_in(ya[:, n]) for n in range(4)]
                         + [lambda n=n: copy_dense(memq[:, n], dense_in()[:, :]) for n in range(4)]
                         + [lambda: copy_dense(skn, dense_in()[:, :]),
                            lambda: copy_dense(sv, dense_in()[:, :].rearrange("p (s d) -> p s d", s=NT))]
                         + [lambda n=n: silu_in(yb[:, n]) for n in range(4)]
                         + [lambda n=n: copy_dense(xq[:, n], dense_in()[:, :]) for n in range(4)]
                         + [lambda n=n: silu_in(yc[:, n]) for n in range(4)])
            act.wait_ge(halves.sem, 1)
            plan = [6, 6, 5, 5]
            for i in range(4):
                if i:
                    act.wait_ge(head_done.sem, i)
                o = a_in()
                do(fn(E[0], o[:, :], ACT.Tanh, bias=col("w0", i, of=half), scale=0.5), decay_th)
                a_read_inc()
                o = a_in()
                do(fn(E[5], o[:, :], ACT.Tanh, bias=col("a0", i, of=half), scale=0.5), decay_th)
                a_read_inc()
                act.wait_ge(decay_ready.sem, i + 1)
                do(fn(E[1], E[2], ACT.Exp))
                do(fn(E[4], E[2], ACT.Exp, scale=-1.0))
                do(fn(E[3], E[3], ACT.Exp))
                do(fn(gexp[:, i, 0:7], gexp[:, i, 0:7], ACT.Exp), exps_ready)
                for _ in range(plan[i]):
                    dense_dst.pop(0)()
            act.wait_ge(head_done.sem, 4)
            norms([memq[:, i, :] for i in range(4)], 1, 1.0 / HD, col("eps6"), refined=True)
            norms([skn], 1, 1.0 / HD, col("eps6"), refined=True)
            norms([xq[:, i, :] for i in range(4)], 1, 1.0 / P, col("eps6"), refined=True)
            norms([km[:, i, :] for i in range(4)], 1, 1.0 / P, col("eps6"), n=M, refined=True)
            attention(window_jobs() + memory_jobs())
            act.wait_ge(o_read.sem, 24)
            for t in range(NT):
                if t:
                    act.wait_ge(mn_ready.sem, 2 * t)
                for dst in (bT, aT[:, :, 0:HD], kT, vT):
                    o = a_in()
                    src = o[:, :] if dst is not None and len(dst.shape) == 2 else o[:, :].rearrange("p (h d) -> p h d", h=8)
                    do(fn(dst, src, ACT.Copy), tm_ready)
                    a_read_inc()
                for hb in range(2):
                    o = a_in()
                    do(fn(aT[:, 4 * hb:4 * hb + 4, HD:P], o[:, 0:4 * HD].rearrange("p (h d) -> p h d", h=4), ACT.Copy), av_ready)
                    a_read_inc()
                    for l in range(1, 6):
                        o = a_in()
                        do(fn(YT, o[:, :], ACT.Copy), y_ready)
                        a_read_inc()
                    o = a_in()
                    if 2 * t + hb:
                        act.wait_ge(mn_ready.sem, 2 * t + hb)
                    do(fn(WU, o[:, :].rearrange("p (h d) -> p h d", h=4), ACT.Copy), wu_ready)
                    a_read_inc()
            act.wait_ge(lnx_ready.sem, 5)
            norms([rwy[:, i, :] for i in range(4)], 1, 1.0 / HD, col("eps_lnx"))
            for j in range(8):
                for g in range(3):
                    o = dense_in()
                    n = 3 * j + g
                    if n >= 6:
                        act.wait_ge(gate_used.sem, n - 5)
                    do(fn(gt[:, n % 6], o[:, :], ACT.Tanh, scale=0.5), dense_act)

            bufs.update(att=(S2, P2, PT2), sq=sq_hi2)
            act.wait_ge(dense_dve.sem, 8)
            norms([x[:, i, :] for i in range(KD)], KD, 1.0 / D, col("eps6"))
            act.wait_ge(mem2_in.sem, 16)
            norms([mem2[:, i, :] for i in range(KD)], KD, 1.0 / D, col("eps6"), n=M)
            act.wait_ge(trig_ready.sem, 2)
            do(fn(trig[:, :, :], trig[:, :, :], ACT.Sin), sin_ready)
            for i in range(4):
                copy_dense(q2[:, i], dense_in()[:, :])
            copy_dense(kraw, dense_in()[:, :])
            for i in range(2):
                copy_dense(qi[:, i], dense_in()[:, :])
            copy_dense(vwi, dense_in()[:, 0:NT * 68].rearrange("p (t d) -> p t d", t=NT))
            for i in range(4):
                if i >= 2:
                    act.wait_ge(u_ready.sem, i - 1)
                do(fn(thg[:, i % 2], dense_in()[:, :], ACT.Tanh, scale=0.5), dense_act)
                do(fn(ga[:, i % 2], dense_in()[:, :], ACT.Copy), glu_ready)
                dense_act_inc()
            for t in range(SEL):
                nk = (2 + t) * P
                for hd in range(4):
                    n = 4 * t + hd
                    o = a_in()
                    if n >= 2:
                        act.wait_ge(rel_used.sem, n - 1)
                    do(fn(rel[:, n % 2, 0:nk], o[:, 0:nk], ACT.Relu, scale=HD ** -0.5), rel_ready)
                    a_read_inc()
            for n in range(8):
                copy_dense(k2[:, n, :], dense_in()[:, 0:M])
            for n in range(8):
                copy_dense(v2[:, :, tok(n)], dense_in()[:, 0:M].rearrange("p (s d) -> p s d", s=2))
            attention(sparse_jobs())
            act.wait_ge(conv_ready.sem, 8)
            norms([mix[:, 4 + i, :] for i in range(4)], 4, 1.0 / 512, col("eps6"))
            for i in range(4):
                act.wait_ge(conv_ready.sem, 9 + i)
                do(fn(tmp[:, i], mix[:, 4 + i, :], ACT.Tanh, bias=col("ln_b_b", i, of=half), scale=col("ln_b_g", i, of=half)), conv_th)
            act.wait_ge(dense_dve.sem, 16)
            norms([x[:, i, :] for i in range(KD)], KD, 1.0 / D, col("eps6"))
            for j in range(8):
                copy_dense(qc[:, j], dense_in()[:, :])
            attention(cross_jobs())
            act.wait_ge(dense_dve.sem, 24)
            norms([x[:, i, :] for i in range(KD)], KD, 1.0 / D, col("eps6"))
            act.wait_ge(ffn_c.sem, 1)
            for f in range(FF + 1):
                if f < FF:
                    o = dense_in()
                    if f >= 2:
                        act.wait_ge(ffn_c.sem, f)
                    do(fn(gpad[:, f % 2, 2:T + 2], o[:, :], ACT.Copy), ffn_g)
                    dense_act_inc()
                if f >= 1:
                    act.wait_ge(ffn_c.sem, f + 1)
                    do(fn(thf[:, (f - 1) % 2], cv[:, (f - 1) % 2], ACT.Tanh, scale=0.5), ffn_th)
                if f < FF:
                    if f >= 2:
                        act.wait_ge(ffn_prod.sem, f - 1)
                    copy_dense(upr[:, f % 2], dense_in()[:, :])
            act.wait_ge(dense_dve.sem, 32)
            norms([x[:, i, :] for i in range(KD)], KD, 1.0 / D, col("eps6"))

        @block.vector
        def _(dve):
            V = nc.vector
            bufs = {"att": (S, Pr, PT), "sq": kk}

            def slot(i):
                return sq[:, i, :] if i < 4 else bufs["sq"][:, i - 4, :]

            def mean_square(i):
                return bufs["att"][i // 2][:, i % 2, :]

            st = {"dense": 0, "v": 0, "proj": 0, "o": 0, "rinv": 0, "att": 0, "exp": 0}
            dense_ids = [g for g, (w, _) in enumerate(groups) if w == "dve"]

            def do(ins, sig=dve_chain):
                sig.inc(ins)
                dve.wait_ge(sig.sem, sig.n)

            def signal_now(sig):
                dve.sem_inc(sig.sem, 1)
                sig.n += 1

            def tt(out, a, b, op, sig=dve_chain):
                do(V.tensor_tensor(out, a, b, op), sig)

            def ts(out, a, s1, s2, o0, o1, sig=dve_chain):
                do(V.tensor_scalar(out, a, s1, s2, o0, o1), sig)

            def ts1(out, a, s1, o0, sig=dve_chain):
                do(V.tensor_scalar(out, a, s1, None, o0), sig)

            def stt(out, a, s, b, o0, o1, sig=dve_chain):
                do(V.scalar_tensor_tensor(out=out, in0=a, scalar=s, in1=b, op0=o0, op1=o1), sig)

            def copy(out, a, sig=dve_chain):
                do(V.tensor_copy(out, a), sig)

            def v_in():
                st["v"] += 1
                dve.wait_ge(v_done.sem, st["v"] - st["proj"])
                return bank[2 + (st["v"] - 1) % 2]

            def proj_in(g):
                st["v"] += 1
                st["proj"] += 1
                dve.wait_ge(dense_done.sem, g + 1)
                return bank[2 + (st["v"] - 1) % 2]

            def rinv_in(i, n=T):
                st["rinv"] += 1
                dve.wait_ge(rinv_ready.sem, st["rinv"])
                return sq[:, i, 0:n]

            def rinv_refined(i, n=T):
                y = rinv_in(i, n)
                t = tmp[:, 0, 0:n]
                tt(t, y, y, MUL)
                tt(t, t, mean_square(i)[:, 0:n], MUL)
                ts(t, t, -0.5, 1.5, MUL, ADD)
                tt(t, t, y, MUL)
                return t

            def angles(src, name, sig, which):
                dve.wait_ge(src.sem, 16)
                copy(tmp[:, 1], tmp[:, 0].bitcast(i32))
                if which:
                    dve.wait_ge(rope_done.sem, 6)
                ts1(tmp[:, 1], tmp[:, 1], col(name), MUL)
                for c in range(2):
                    ts(tmp[:, 2], tmp[:, 1], 1 / (2 * math.pi), 0.25 * c, MUL, ADD)
                    ts(tmp[:, 2], tmp[:, 2], ROUND, ROUND, ADD, SUB)
                    a = tmp[:, 1]
                    for part in TWO_PI:
                        stt(tmp[:, 3], tmp[:, 2], -part, a, MUL, ADD)
                        a = tmp[:, 3]
                    if c:
                        ts1(tmp[:, 3], tmp[:, 3], col("half_pi"), ADD)
                    ts(trig[:, c], tmp[:, 3], math.pi - 4e-7, -math.pi + 4e-7, MIN, MAX, sig if c else dve_chain)

            def apply_norm(g, n=T, tiles=KD, src=x, dst=h, per_tile=None):
                ri = rinv_in(0, n)
                for i in range(tiles):
                    stt(dst[:, i, :], src[:, i, :], col(g, i), ri, MUL, MUL,
                        norm_applied if i == tiles - 1 else (per_tile or dve_chain))

            def rope(dst, src):
                tt(tmp[:, 0], src, trig[:, 1], MUL)
                o = v_in()
                tt(tmp[:, 1], o[:, :], trig[:, 0], MUL, v_read)
                tt(dst, tmp[:, 0], tmp[:, 1], ADD, rope_done)

            def rope_dup(dst):
                o = v_in()
                tt(tmp[:, 0], o[:, :], trig[:, 1], MUL, v_read)
                o = v_in()
                tt(tmp[:, 1], o[:, :], trig[:, 0], MUL, v_read)
                tt(dst, tmp[:, 0], tmp[:, 1], ADD, rope_done)

            def attention(jobs):
                n = len(jobs)
                for i in range(n + 2):
                    if i < n:
                        nk, scale, score, mask, sinks, *_ = jobs[i]
                        U = len(score)
                        w = U * nk
                        o = v_in()
                        s = st["att"] % 2
                        st["att"] += 1
                        sc_ = bufs["att"][0][:, s, 0:w]
                        sc3 = sc_.rearrange("p (u n) -> p u n", u=U)
                        if mask is None:
                            copy(sc_, o[:, 0:w], v_read)
                        else:
                            tt(sc3, o[:, 0:w].rearrange("p (u n) -> p u n", u=U),
                               mask.unsqueeze(1).broadcast_to([P, U, nk]), ADD, v_read)
                        mx, nb_ = small[:, s, 0:U], small[:, s, 2:2 + U]
                        do(V.reduce_max(mx, sc3, AX))
                        if sinks is None:
                            ts1(nb_, mx, -scale, MUL, bias_ready)
                        else:
                            stt(mx, mx, scale, sinks, MUL, MAX)
                            ts1(nb_, mx, -1.0, MUL, bias_ready)
                    if 1 <= i <= n:
                        nk, scale, score, mask, sinks, *_ = jobs[i - 1]
                        U = len(score)
                        s = st["exp"] % 2
                        st["exp"] += 1
                        dve.wait_ge(exp_done.sem, st["exp"])
                        den = small[:, s, 4:4 + U]
                        if sinks is not None:
                            tt(den, den, small[:, s, 6:6 + U], ADD)
                        do(V.reciprocal(small[:, s, 8:8 + U], den))
                        for u_ in range(U):
                            pb = bufs["att"][1][:, s, u_ * nk:(u_ + 1) * nk]
                            ts1(pb, pb, small[:, s, 8 + u_:9 + u_], MUL, p_ready if u_ == U - 1 else dve_chain)
                    if i >= 2:
                        _, _, _, _, _, _, view, dst, gate = jobs[i - 2]
                        st["o"] += 1
                        dve.wait_ge(o_done.sem, st["o"])
                        o = view(bank[6 + (st["o"] - 1) % 2])
                        if gate is None:
                            copy(dst, o, o_read)
                        else:
                            tt(dst, o, gate, MUL, o_read)

            dve.wait_ge(cols_in.sem, 16)
            ts1(half[:, :], cols[:, :], 0.5, MUL, halves)
            for s in range(2):
                do(V.memset(raw[:, s, 0:1], 0.0), raw_used if s else dve_chain)
            angles(pos_in, "freq", trig_ready, 0)
            for i in range(4):
                dve.wait_ge(x_in[i].sem, 16)
            apply_norm("norm_g")
            dve.wait_ge(mem_in.sem, 16)
            apply_norm("mem_norm_g", M, KD, mem, mem)
            for n in range(13):
                dve.wait_ge(raw_ready.sem, n + 1)
                cur, prev = raw[:, n % 2, 1:T + 1], raw[:, n % 2, 0:T]
                dst = [r, k, v][n // 4][:, n % 4, :] if n < 12 else lwa
                tt(tmp[:, 0], prev, cur, SUB)
                stt(dst, tmp[:, 0], col("mu", n), cur, MUL, ADD, raw_used)
            for i in range(4):
                ri = rinv_in(i)
                ts1(tmp[:, 0], ri, 1e12, MIN)
                stt(kk[:, i, :], k[:, i, :], col("k_k", i), tmp[:, 0], MUL, MUL, norm_applied)
            for i in range(4):
                dve.wait_ge(decay_th.sem, 2 * i + 1)
                half_decay = -0.5 * EXP_HALF
                ts(E[0], E[0], half_decay, half_decay, MUL, ADD)
                dve.wait_ge(cst_in.sem, 16)
                do(V.tensor_tensor_scan(E[1], con("restart", 0, T), E[0], 0.0, MUL, ADD))
                sums = E[1].rearrange("p (c t) -> p c t", t=C)
                tt(gexp[:, i, 0:7], sums[:, 0:7, C - 1], sums[:, 0:7, C // 2 - 1], SUB)
                tt(gexp[:, i, 0:7], gexp[:, i, 0:7], sums[:, 1:8, C // 2 - 1], ADD)
                tt(E[2].rearrange("p (c t) -> p c t", t=C), sums, sums[:, :, C // 2 - 1:C // 2].broadcast_to([P, T // C, C]), SUB)
                dve.wait_ge(decay_th.sem, 2 * i + 2)
                tt(E[3], E[2], E[0], SUB, decay_ready)
                ts(E[5], E[5], 0.5, 0.5, MUL, ADD)
                ts(tmp[:, 0], E[5], -1.0, col("k_a", i), ADD, MUL)
                stt(k[:, i, :], tmp[:, 0], 1.0, k[:, i, :], ADD, MUL)
                stt(E[0], r[:, i, :], col("r_k", i), k[:, i, :], MUL, MUL, rk_ready)
                tt(bb[:, i, :], kk[:, i, :], E[5], MUL)
                dve.wait_ge(exps_ready.sem, i + 1)
                stt(kk[:, i, :], kk[:, i, :], -1.0, E[3], MUL, MUL)
                tt(bb[:, i, :], bb[:, i, :], E[4], MUL)
                tt(k[:, i, :], k[:, i, :], E[4], MUL)
                tt(r[:, i, :], r[:, i, :], E[1], MUL)
                o = v_in()
                tt(bonus[:, i, :], o[:, :], v[:, i, :], MUL, v_read)
                signal_now(head_done)
            for i in range(4):
                ri = rinv_refined(i)
                stt(memq[:, i, :], memq[:, i, :], col("q_g"), ri, MUL, MUL, norm_applied)
                signal_now(rope_in)
            ri = rinv_refined(0)
            stt(skn, skn, col("k_g"), ri, MUL, MUL, norm_applied)
            signal_now(rope_in)
            dve.wait_ge(sin_ready.sem, 1)
            for i in range(4):
                rope(memq[:, i, :], memq[:, i, :])
            for s in range(2):
                rope_dup(skd[:, s, :])
            for i in range(4):
                ri = rinv_refined(i)
                stt(xq[:, i, :], xq[:, i, :], col("xq_g"), ri, MUL, MUL, norm_applied)
            for i in range(4):
                ri = rinv_refined(i, M)
                stt(km[:, i, :], km[:, i, :], col("xk_g"), ri, MUL, MUL, norm_applied)
            dve.wait_ge(silu_done.sem, 12)
            attention(window_jobs() + memory_jobs())

            for t in range(NT):
                for hb in range(2):
                    j4 = "p (j t) -> p j t"
                    b4 = [P, 4, P]
                    if 2 * t + hb:
                        dve.wait_ge(wu_ready.sem, 2 * t + hb)
                    lev = con("level0").unsqueeze(1).broadcast_to(b4)
                    levT = con("levelT", 0).unsqueeze(1).broadcast_to(b4)
                    strict = con("strictT").unsqueeze(1).broadcast_to(b4)
                    incl = con("inclT").unsqueeze(1).broadcast_to(b4)
                    eye = con("ident").unsqueeze(1).broadcast_to(b4)

                    def f4(a):
                        return a.rearrange(j4, j=4)
                    o = v_in()
                    tt(f4(tmp[:, 0]), f4(o[:, :]), lev, MUL, v_read)
                    tt(f4(XX), f4(tmp[:, 0]), eye, ADD)
                    o = v_in()
                    tt(f4(tmp[:, 0]), f4(o[:, :]), levT, MUL)
                    if 2 * t + hb:
                        dve.wait_ge(ml_ready.sem, 5 * (2 * t + hb))
                    tt(f4(AB), f4(o[:, :]), strict, MUL, v_read)
                    tt(f4(XT), f4(tmp[:, 0]), eye, ADD, gram_ready)
                    o = v_in()
                    tt(f4(AK), f4(o[:, :]), strict, MUL, v_read)
                    signal_now(gram_ready)
                    o = v_in()
                    tt(f4(RB), f4(o[:, :]), incl, MUL, v_read)
                    o = v_in()
                    tt(f4(RK), f4(o[:, :]), incl, MUL, v_read)
                    signal_now(gram_ready)
                    for l in range(1, 6):
                        if l < 5:
                            o = v_in()
                            tt(XX, XX, o[:, :], ADD, v_read)
                        o = v_in()
                        tt(XT, XT, o[:, :], ADD, v_read)
                        signal_now(inv_ready)
                    rs = r[:, 2 * hb:2 * hb + 2, tok(t)]
                    o = v_in()
                    tt(rs, rs, o[:, 0:2 * P].rearrange("p (i t) -> p i t", i=2), ADD, v_read)
                    o = v_in()
                    copy(rwy[:, 2 * hb:2 * hb + 2, tok(t)], o[:, 0:2 * P].rearrange("p (i t) -> p i t", i=2), v_read)
                    o = v_in()
                    eye64 = con("ident64", 0, HD).unsqueeze(1).broadcast_to([P, 4, HD])
                    tt(tmp[:, 1, 0:4 * HD].rearrange("p (q d) -> p q d", q=4), o[:, 0:4 * HD].rearrange("p (q d) -> p q d", q=4), eye64, ADD, v_read)
                    mt = MT[:, :, 2 * hb * HD:2 * (hb + 1) * HD]
                    copy(mt, tmp[:, 1, 0:4 * HD].rearrange("p (c d) -> p c d", c=2))
                    o = v_in()
                    copy(NN[:, :, 2 * hb * HD:2 * (hb + 1) * HD], o[:, 0:4 * HD].rearrange("p (c d) -> p c d", c=2), v_read)
                    signal_now(mn_ready)
                for c in range(2):
                    cc = 2 * t + c
                    src = NN[:, c]
                    if cc:
                        o = v_in()
                        ys = rwy[:, :, tok(cc, C)]
                        tt(ys, ys, o[:, 0:4 * C].rearrange("p (i t) -> p i t", i=4), ADD, v_read)
                        if cc < 7:
                            o = v_in()
                            tt(tmp[:, 2, 0:4 * HD], o[:, 0:4 * HD], NN[:, c], ADD, v_read)
                            src = tmp[:, 2, 0:4 * HD]
                    if cc < 7:
                        tt(St[:, (cc + 1) % 2].rearrange("p (i d) -> p i d", i=4), src.rearrange("p (i d) -> p i d", i=4),
                           gexp[:, :, cc:cc + 1].broadcast_to([P, 4, HD]), MUL, state_ready)
            signal_now(lnx_ready)
            for i in range(4):
                o = v_in()
                stt(rwy[:, i, :], o[:, :], -1.0 / HD, rwy[:, i, :], MUL, ADD, v_read)
                signal_now(lnx_ready)
            for i in range(4):
                ri = rinv_in(i)
                stt(tmp[:, 0], rwy[:, i, :], col("lnx_g", i), ri, MUL, MUL)
                stt(tmp[:, 0], tmp[:, 0], col("lnx_b", i), bonus[:, i, :], ADD, ADD)
                tt(ya[:, i, :], tmp[:, 0], ya[:, i, :], MUL, norm_applied)
            for j in range(8):
                for g in range(3):
                    o = proj_in(13 + 8 + 22 + 6 * j + 3 + g)
                    dve.wait_ge(dense_act.sem, 13 + 8 + 22 + 3 * j + g + 1)
                    stt(tmp[:, g], gt[:, (3 * j + g) % 6], 1.0, o[:, :], ADD, MUL, v_read)
                    signal_now(gate_used)
                tt(tmp[:, 0], tmp[:, 0], tmp[:, 1], ADD)
                tt(merged[:, j, :], tmp[:, 0], tmp[:, 2], ADD, merged_ready)

            def dense_in():
                g = dense_ids[st["dense"]]
                dve.wait_ge(dense_done.sem, g + 1)
                st["dense"] += 1
                return bank[uses[g] % 2]

            def add_dense(s=1.0):
                for j in range(KD):
                    o = dense_in()
                    stt(x[:, j, :], o[:, :], s, x[:, j, :], MUL, ADD, dense_dve)

            add_dense(0.5)
            signal_now(block1_done)

            bufs.update(att=(S2, P2, PT2), sq=sq_hi2)
            angles(pos2_in, "freq2", trig_ready, 1)
            for s in range(4):
                do(V.memset(u[:, s, 0:TAPS - 1], 0.0), u_zero if s == 3 else dve_chain)
            apply_norm("norm_mix_g")
            dve.wait_ge(mem2_in.sem, 16)
            apply_norm("norm_mem_g", M, KD, mem2, mem2)
            dve.wait_ge(sin_ready.sem, 2)
            dve.wait_ge(dense_act.sem, DQ + 8)
            for i in range(4):
                rope(q2[:, i, :], q2[:, i, :])
            for i in range(2):
                rope(qi[:, i, :], qi[:, i, :])
            rope_dup(kd)
            rope_dup(kid)
            for t in range(NT):
                ts1(vwi[:, t, HD:HD + 4], vwi[:, t, HD:HD + 4], 0.5, MUL)
            for t in range(SEL):
                nk = (2 + t) * P
                for hd in range(4):
                    n = 4 * t + hd
                    dve.wait_ge(rel_ready.sem, n + 1)
                    w = vwi[:, 1 + t, HD + hd:HD + hd + 1]
                    if hd == 0:
                        ts1(sc[:, t, 0:nk], rel[:, n % 2, 0:nk], w, MUL, rel_used)
                    else:
                        stt(sc[:, t, 0:nk], rel[:, n % 2, 0:nk], w, sc[:, t, 0:nk], MUL, ADD, rel_used)
                tt(sc[:, t, nk - P:nk], sc[:, t, nk - P:nk], con("causal", 1), ADD)
            for rnd in range(TOPK // 8):
                for t in range(SEL):
                    nk = (2 + t) * P
                    do(V.max(max8[:, t, :], sc[:, t, 0:nk]))
                    do(V.match_replace(sc[:, t, 0:nk], max8[:, t, :], sc[:, t, 0:nk], TAKEN))
            for t in range(SEL):
                nk = (2 + t) * P
                ts(sel[:, t, 0:nk], sc[:, t, 0:nk], -3e38, MASKED, ALU.is_gt, MUL)
            attention(sparse_jobs())
            for i in range(4):
                dve.wait_ge(u_ready.sem, i + 1)
                acc = mix[:, 4 + i, :]
                ts(acc, u[:, i, 0:T], col("conv_w", i * TAPS), col("conv_b", i), MUL, ADD)
                for w in range(1, TAPS):
                    stt(acc, u[:, i, w:w + T], col("conv_w", i * TAPS + w), acc, MUL, ADD,
                        conv_ready if w == TAPS - 1 else dve_chain)
            o = v_in()
            copy(tmp[:, 0], o[:, :], v_read)
            for i in range(4):
                stt(mix[:, 4 + i, :], tmp[:, 0], -1.0 / 512, mix[:, 4 + i, :], MUL, ADD, conv_ready)
            ri = rinv_in(0)
            for i in range(4):
                tt(mix[:, 4 + i, :], mix[:, 4 + i, :], ri, MUL, conv_ready)
            signal_now(norm_applied)
            for i in range(4):
                dve.wait_ge(conv_th.sem, i + 1)
                ts(mix[:, 4 + i, :], mix[:, 4 + i, :], col("ln_b_g", i, of=half), col("ln_b_b", i, of=half), MUL, ADD)
                stt(mix[:, 4 + i, :], tmp[:, i], 1.0, mix[:, 4 + i, :], ADD, MUL, mix_ready)
            add_dense()
            apply_norm("norm_cross_g")
            attention(cross_jobs())
            add_dense()
            apply_norm("norm_ffn_g")
            do(V.memset(gpad[:, :, 0:FTAPS - 1], 0.0), ffn_c)
            for f in range(FF + 1):
                if f < FF:
                    dve.wait_ge(ffn_g.sem, f + 1)
                    s = f % 2
                    ts(cv[:, s], gpad[:, s, 0:T], col("ffn_w", f * FTAPS), col("ffn_b", f), MUL, ADD)
                    stt(cv[:, s], gpad[:, s, 1:T + 1], col("ffn_w", f * FTAPS + 1), cv[:, s], MUL, ADD)
                    stt(cv[:, s], gpad[:, s, 2:T + 2], col("ffn_w", f * FTAPS + 2), cv[:, s], MUL, ADD, ffn_c)
                if f >= 1:
                    s = (f - 1) % 2
                    dve.wait_ge(ffn_th.sem, f)
                    stt(tmp[:, 0], thf[:, s], 1.0, cv[:, s], ADD, MUL)
                    dve.wait_ge(dense_act.sem, DF + 2 * f)
                    tt(prod[:, f - 1, :], tmp[:, 0], upr[:, s], MUL, ffn_prod)
            add_dense(0.5)
            ri = rinv_in(0)
            for i in range(KD):
                stt(h[:, i, :], x[:, i, :], col("norm_final_g", i), ri, MUL, MUL, x_final)

        @block.gpsimd
        def _(pool):
            G = nc.gpsimd

            def do(ins, sig=pool_chain):
                sig.inc(ins)
                pool.wait_ge(sig.sem, sig.n)

            dst = [y[:, n] for y in (ya, yb, yc) for n in range(4)]
            for n in range(12):
                pool.wait_ge(th_ready.sem, n + 1)
                do(G.tensor_scalar(thz[:, n % 2], thz[:, n % 2], 1.0, None, ADD))
                do(G.tensor_tensor(dst[n], dst[n], thz[:, n % 2], MUL), silu_done)
            n = 0
            for t in range(NT):
                for hb in range(2):
                    pool.wait_ge(gram_ready.sem, 3 * (2 * t + hb) + 1)
                    for l in range(1, 6):
                        n += 1
                        if n > 2:
                            pool.wait_ge(y_ready.sem, n - 2)
                        lev = con("levelT", l).unsqueeze(1).broadcast_to([P, 4, P])
                        do(G.tensor_tensor(ML[:, n % 2].rearrange("p (j t) -> p j t", j=4), AB.rearrange("p (j t) -> p j t", j=4), lev, MUL), ml_ready)
            pool.wait_ge(block1_done.sem, 1)
            pool.dma_start(tmp[:, 0].bitcast(i32), pos2_d).then_inc(pos2_in.sem, 16)
            pool.dma_start(mem2, mem2t).then_inc(mem2_in.sem, 16)
            pool.wait_ge(u_zero.sem, 1)
            for i in range(4):
                pool.wait_ge(glu_ready.sem, i + 1)
                do(G.tensor_scalar(thg[:, i % 2], thg[:, i % 2], 0.5, 0.5, MUL, ADD))
                do(G.tensor_tensor(u[:, i, TAPS - 1:TAPS - 1 + T], thg[:, i % 2], ga[:, i % 2], MUL), u_ready)


        @block.sync
        def _(sp):
            for i in range(4):
                sp.dma_start(x[:, 2 * i:2 * i + 2, :], xt[:, 2 * i:2 * i + 2, :]).then_inc(x_in[i].sem, 16)
            for p in range(NPANEL):
                if p >= RING:
                    sp.wait_ge(dense_done.sem, last_user[p - RING])
                sp.dma_start(ring[:, p % RING], weights[p]).then_inc(panel_in[p % RING].sem, 16)
            for i in range(KD):
                sp.wait_ge(x_final.sem, i + 1)
                sp.dma_start(out_d[:, i, :], h[:, i, :]).then_inc(out_done.sem, 16)
            sp.wait_ge(out_done.sem, 16 * KD)


def kernel(**inputs):
    import concourse.bacc as bacc
    from concourse.bass_utils import run_bass_kernel_spmd

    a = {n: np.asarray(v) for n, v in inputs.items()}

    def tiles(m):
        return np.ascontiguousarray(m.T.reshape(-1, P, m.shape[0]).transpose(1, 0, 2))

    def blocks(w, order=None):
        k, n = w.shape
        b = w.reshape(k // P, P, n // P, P).transpose(2, 0, 1, 3)
        return b if order is None else b[order]

    w_in, w_in2 = blocks(a["w_in"][0]), a["w_in_2"][0]
    q, kp, vp, qip, kip, wip, glu = np.split(w_in2, np.cumsum([512, 64, 64, 256, 64, 4]), axis=1)
    pad = np.zeros((D, 60), np.float32)
    w_in2 = blocks(np.concatenate([q, kp, kip, qip, vp, wip, pad], 1))
    ga, gg = blocks(glu[:, :512]), blocks(glu[:, 512:])
    pa, pb, pc = (blocks(a[n][0]) for n in ("w_proj_a", "w_proj_b", "w_proj_c"))
    parts = [w_in[0:13], blocks(a["w_mem_kv"][0]), w_in[13:35]]
    for j in range(8):
        parts += [w_in[35 + j], w_in[43 + j], w_in[51 + j], pa[j], pb[j], pc[j]]
    parts += [blocks(a["w_out"][0]), w_in2]
    for j in range(4):
        parts += [gg[j], ga[j]]
    parts += [blocks(a[n][0]) for n in ("w_k_cross_2", "w_v_cross_2", "w_out_2", "w_q_cross_2", "w_o_cross_2")]
    wg, wu = blocks(a["w_gate_2"][0]), blocks(a["w_up_2"][0])
    for f in range(FF):
        parts += [wg[f], wu[f]]
    parts.append(blocks(a["w_down_2"][0]))
    stream = np.concatenate([p.reshape(-1, P, P) for p in parts])
    weights = np.ascontiguousarray(stream.reshape(-1, PB, P, P).transpose(0, 2, 1, 3))

    cols = np.zeros((P, NCOLS), np.float32)

    def put(name, v):
        o, n = COLS[name]
        cols[:, o:o + n] = v

    def per_feature(v):
        return v.reshape(-1, P).T

    for name in ("norm_g", "mem_norm_g", "w0", "a0", "k_k", "k_a", "lnx_g", "lnx_b"):
        put(name, per_feature(a[name][0]))
    put("mu", per_feature(np.concatenate([a["mu_rkv"][0].reshape(-1), a["mu_wa"][0].reshape(-1)])))
    put("r_k", per_feature(a["r_k"][0].reshape(-1)))
    for name, src in (("q_g", "q_norm_g"), ("k_g", "k_norm_g")):
        put(name, np.tile(a[src][0], 2)[:, None])
    put("xq_g", a["xq_norm_g"][0][:, None])
    put("xk_g", a["xk_norm_g"][0][:, None])
    put("sinks", np.broadcast_to(a["sinks"][0], (P, 8)))
    for name in ("norm_mix_g", "norm_cross_g", "norm_mem_g", "norm_ffn_g", "ln_b_g", "ln_b_b"):
        put(name, per_feature(a[name + "_2"][0]))
    put("norm_final_g", per_feature(a["norm_final_g_2"]))
    put("conv_w", a["conv_b_w_2"][0].T.reshape(4, P, TAPS).transpose(1, 0, 2).reshape(P, -1))
    put("conv_b", per_feature(a["conv_b_b_2"][0]))
    put("ffn_w", a["ffn_conv_w_2"][0].T.reshape(FF, P, FTAPS).transpose(1, 0, 2).reshape(P, -1))
    put("ffn_b", per_feature(a["ffn_conv_b_2"][0]))
    d = np.arange(P) % HD
    put("freq", (10000.0 ** (-(d % 32) / 32))[:, None])
    put("freq2", np.where(d < 16, 500000.0 ** (-2.0 * (d % 8) / 16), 0.0)[:, None])
    for name, value in (("eps6", 1e-6), ("eps_lnx", 64e-5), ("kk_eps", 2.0 ** -64),
                        ("kk_bias", LN_SHIFT / 2 * math.log(2)), ("half_pi", math.pi / 2)):
        put(name, value)

    arrays = {
        "xt": tiles(a["x"][0]), "memt": tiles(a["mem"][0]), "mem2t": tiles(a["mem_2"][0]),
        "weights": weights, "cols_in": cols, "cst_in": constants(),
        "wa2": np.ascontiguousarray(np.concatenate([a["w2"][0], a["a2"][0]])),
        "pos": np.ascontiguousarray(np.broadcast_to(a["positions"], (P, T))),
        "pos2": np.ascontiguousarray(np.broadcast_to(a["positions_2"], (P, T))),
    }
    nc = bacc.Bacc("TRN2", target_bir_lowering=False, num_devices=1)
    aps = [nc.dram_tensor(n, v.shape, mybir.dt.from_np(v.dtype), kind="ExternalInput").ap() for n, v in arrays.items()]
    out = nc.dram_tensor("out", (P, KD, T), mybir.dt.float32, kind="ExternalOutput").ap()
    build(nc, *aps, out)
    res = run_bass_kernel_spmd(nc, [arrays], core_ids=[0]).results[0]["out"]
    return np.ascontiguousarray(res.transpose(1, 0, 2).reshape(D, T).T)[None]
```

```python
import math
from contextlib import ExitStack

import numpy as np
import concourse.bass as bass
from concourse import mybir

P = 128
T = 512
NT = T // P
D = 1024
KD = D // P
M = 256
HD = 64
C = 64
RW = 4
FF = 2816 // P
TAPS, FTAPS = 31, 3
TOPK = min(256, T // 4)
SEL = NT - 1
RING = 4
PB = 8
MASKED = -1e30
TAKEN = -3.3e38
EXP_HALF = math.exp(-0.5)
LN_SHIFT = 30
TWO_PI = (6.28125, 1014.0 / 2 ** 19, 2 * math.pi - 6.28125 - 1014.0 / 2 ** 19)
ROUND = 1.5 * 2 ** 23

COLS = {}
for _name, _n in (("norm_g", 8), ("mem_norm_g", 8), ("mu", 13), ("w0", 4), ("a0", 4), ("k_k", 4), ("k_a", 4),
                  ("r_k", 4), ("lnx_g", 4), ("lnx_b", 4), ("q_g", 1), ("k_g", 1), ("xq_g", 1), ("xk_g", 1),
                  ("sinks", 8), ("norm_mix_g", 8), ("norm_cross_g", 8), ("norm_mem_g", 8), ("norm_ffn_g", 8),
                  ("norm_final_g", 8), ("ln_b_g", 4), ("ln_b_b", 4), ("conv_w", 4 * TAPS), ("conv_b", 4),
                  ("ffn_w", FF * FTAPS), ("ffn_b", FF),
                  ("freq", 1), ("freq2", 1), ("eps6", 1), ("eps_lnx", 1), ("zero", 1), ("kk_eps", 1), ("kk_bias", 1),
                  ("half_pi", 1)):
    COLS[_name] = (sum(n for _, n in COLS.values()), _n)
NCOLS = sum(n for _, n in COLS.values())

CST = {}
for _name, _n in (("ones", P), ("head_ones", P), ("ident", P), ("ident64", HD), ("rot", P), ("dup0", P), ("dup1", P),
                  ("rotdup0", P), ("rotdup1", P), ("rot2", P), ("rot2dup0", P), ("rot2dup1", P),
                  ("level0", P), ("levelT", 6 * P), ("strictT", P), ("inclT", P), ("causal", 2 * P),
                  ("band", 2 * P), ("restart", T)):
    CST[_name] = (sum(n for _, n in CST.values()), _n)
NCST = sum(n for _, n in CST.values())


def constants():
    c = np.zeros((P, NCST), np.float32)

    def put(name, a):
        o, n = CST[name]
        c[:, o:o + n] = a.reshape(P, n)

    i = np.arange(P)
    row, col = i[:, None], i[None, :]
    put("ones", np.ones((P, P)))
    put("head_ones", (row // HD == col // HD) * 1.0)
    put("ident", np.eye(P))
    put("ident64", np.concatenate([np.eye(HD)] * 2))

    def rotation(half):
        r = np.zeros((P, P))
        for m in range(P):
            d = m % HD
            if d < half:
                r[m + half, m] = -1
            elif d < 2 * half:
                r[m - half, m] = 1
        return r

    dup = []
    for s in range(2):
        d = np.zeros((P, P))
        for m in range(P):
            d[s * HD + m % HD, m] = 1
        dup.append(d)
    put("rot", rotation(HD // 2))
    put("rot2", rotation(8))
    for s in range(2):
        put(f"dup{s}", dup[s])
        put(f"rotdup{s}", dup[s] @ rotation(HD // 2))
        put(f"rot2dup{s}", dup[s] @ rotation(8))
    levels = []
    for l in range(6):
        s = 1 << l
        levels.append((row // (2 * s) == col // (2 * s)) & ((row // s) % 2 == 1) & ((col // s) % 2 == 0))
    put("level0", levels[0] * 1.0)
    put("levelT", np.stack([m.T for m in levels], 1) * 1.0)
    put("strictT", ((row < col) & (row // C == col // C)) * 1.0)
    put("inclT", ((row <= col) & (row // C == col // C)) * 1.0)
    after = np.where(col > row, MASKED, 0.0)
    put("causal", np.concatenate([np.zeros((P, P)), after], 1))
    put("band", np.concatenate([np.where(col > row, 0.0, MASKED), after], 1))
    put("restart", np.broadcast_to((np.arange(T) % C != 0) * 1.0, (P, T)))
    return c


class Signal:

    def __init__(self, sem):
        self.sem, self.n = sem, 0

    def inc(self, ins):
        ins.then_inc(self.sem, 1)
        self.n += 1


def build(nc, xt, memt, mem2t, weights, cols_d, cst_d, wa2_d, pos_d, pos2_d, out_d):
    f32 = mybir.dt.float32
    i32 = mybir.dt.int32
    ALU = mybir.AluOpType
    ACT = mybir.ActivationFunctionType
    AX = mybir.AxisListType.X
    ADD, SUB, MUL, MAX, MIN = ALU.add, ALU.subtract, ALU.mult, ALU.max, ALU.min

    with ExitStack() as ctx:
        def sb(name, shape, dt=f32):
            return ctx.enter_context(nc.sbuf_tensor(name, shape, dt))

        def signal(name):
            return Signal(ctx.enter_context(nc.semaphore(name)))

        x = sb("x", [P, KD, T])
        h = sb("h", [P, KD, T])
        ring = sb("ring", [P, RING, PB, P])
        cst = sb("cst", [P, NCST])
        cols = sb("cols", [P, NCOLS])
        half = sb("half", [P, NCOLS])
        trig = sb("trig", [P, 2, T])
        sq = sb("sq", [P, 4, T])
        tmp = sb("tmp", [P, 4, T])
        small = sb("small", [P, 2, 16])
        ARENA = 31300
        arena = sb("arena", [P, ARENA])
        top = [0]

        def take(*shape):
            n = int(np.prod(shape))
            a = arena[:, top[0]:top[0] + n]
            top[0] += n
            assert top[0] <= ARENA, (top, shape)
            names = "abc"[:len(shape)]
            if len(shape) == 1:
                return a
            return a.rearrange(f"p ({' '.join(names)}) -> p {' '.join(names)}",
                               **{m: s for m, s in zip(names[1:], shape[1:])})

        ya, yb, yc = take(4, T), take(4, T), take(4, T)
        r, k, v = take(4, T), take(4, T), take(4, T)
        kk, bb = take(4, T), take(4, T)
        bonus = take(4, T)
        mem = take(KD, M)
        memq = mem.rearrange("p a b -> p (a b)").rearrange("p (a b) -> p a b", a=4)
        arena2 = top[0]
        wa2 = bonus[:, 3, :]
        xq, km, vm = take(4, T), take(4, M), take(2, T)
        skd, sv = take(2, T), take(NT, P)
        S, Pr, PT = take(2, T), take(2, T), take(2, T)
        raw = take(2, 514)
        skn = skd[:, 1, :]
        thz = take(2, T)
        lwa = thz[:, 0]
        E = [S[:, 0], S[:, 1], Pr[:, 0], Pr[:, 1], PT[:, 0], PT[:, 1]]
        gexp = sb("gexp", [P, 4, 8])
        end_attn = top[0]
        top[0] = arena2
        bT, kT, vT = take(T), take(T), take(T)
        aT = take(8, P)
        AB, AK, RB, RK = take(T), take(T), take(T), take(T)
        XX, XT, YT = take(T), take(T), take(T)
        ML = take(2, T)
        WU = take(4, P)
        MT, NN = take(2, 4 * HD), take(2, 4 * HD)
        St = take(2, 4 * HD)
        late = take(2, T)
        top[0] = max(top[0], end_attn)
        partial = [sq[:, 0], sq[:, 1], sq[:, 2], sq[:, 3], trig[:, 0], trig[:, 1], late[:, 0], late[:, 1]]
        gt = [tmp[:, 3], thz[:, 1]]
        gn_sq = arena[:, arena2:arena2 + 4 * T].rearrange("p (a b) -> p a b", a=4)
        rwy = memq
        gates_a = arena[:, 3 * 2048:5 * 2048].rearrange("p (a b) -> p a b", a=8)
        merged = arena[:, 5 * 2048:7 * 2048].rearrange("p (a b) -> p a b", a=8)
        top[0] = 0
        mem2 = take(KD, M)
        k2, v2 = take(KD, M), take(2, D)
        mix = take(8, T)
        q2, qi, kd, kid = take(4, T), take(2, T), take(T), take(T)
        vwi = take(NT, 68)
        sc, sel = take(SEL, T), take(SEL, T)
        rel = take(2, T)
        u = take(4, TAPS - 1 + T)
        thg, ga = take(2, T), take(2, T)
        kraw = take(T)
        S2, P2, PT2 = take(2, T), take(2, T), take(2, T)
        max8 = sb("max8", [P, SEL, 8])
        sq_hi2 = take(4, T)
        top[0] = 3 * 2048
        qc, oc = take(8, T), take(8, T)
        top[0] = 0
        prod = take(FF, T)
        gpad = take(2, T + FTAPS - 1)
        upr, cv, thf = take(2, T), take(2, T), take(2, T)

        bank = [ctx.enter_context(nc.psum_tensor(f"bank{i}", [P, T], f32)) for i in range(8)]

        def col(name, i=0, n=1, of=cols):
            o, m = COLS[name]
            assert i + n <= m
            return of[:, o + i:o + i + n]

        def con(name, i=0, n=P):
            o, m = CST[name]
            return cst[:, o + i * n:o + (i + 1) * n]

        def tok(t, n=P):
            return slice(t * n, (t + 1) * n)

        panel_in = [signal(f"panel_in{s}") for s in range(RING)]
        x_in = [signal(f"x_in{i}") for i in range(4)]
        cst_in, cols_in, wa2_in, pos_in, pos2_in, mem_in, mem2_in, out_done = (signal(n) for n in (
            "cst_in", "cols_in", "wa2_in", "pos_in", "pos2_in", "mem_in", "mem2_in", "out_done"))
        dense_done = signal("dense_done")
        dense_act, dense_dve = signal("dense_read_by_act"), signal("dense_read_by_dve")
        v_done, v_read = signal("vbank_done"), signal("vbank_read")
        a_done, a_read = signal("abank_done"), signal("abank_read")
        o_done, o_read = signal("obank_done"), signal("obank_read")
        act_chain, dve_chain, pool_chain = signal("act_chain"), signal("dve_chain"), signal("pool_chain")
        halves, trig_ready = signal("halves"), signal("trig_ready")
        sq_ready, rinv_ready, norm_applied = signal("sq_ready"), signal("rinv_ready"), signal("norm_applied")
        raw_ready, raw_used = signal("raw_ready"), signal("raw_used")
        lora_ready, decay_ready, exps_ready, head_done, rk_ready = (signal(n) for n in (
            "lora_ready", "decay_ready", "exps_ready", "head_done", "rk_ready"))
        th_ready, silu_done = signal("th_ready"), signal("silu_done")
        rope_in, rope_done = signal("rope_in"), signal("rope_done")
        bias_ready, exp_done, p_ready, pt_ready = (signal(n) for n in ("bias_ready", "exp_done", "p_ready", "pt_ready"))
        tm_ready, gram_ready, ml_ready, ml_free, wu_ready, state_ready, y_ready = (signal(n) for n in (
            "tm_ready", "gram_ready", "ml_ready", "ml_free", "wu_ready", "state_ready", "y_ready"))
        inv_ready, mn_ready, av_ready = signal("inv_ready"), signal("mn_ready"), signal("av_ready")
        lnx_ready = signal("lnx_ready")
        merged_ready, gate_used = signal("merged_ready"), signal("gate_used")
        block1_done, glu_ready, glu_used, u_ready = (signal(n) for n in ("block1_done", "glu_ready", "glu_used", "u_ready"))
        rel_ready, rel_used = signal("rel_ready"), signal("rel_used")
        conv_ready, mix_ready, conv_th = signal("conv_ready"), signal("mix_ready"), signal("conv_th")
        ffn_g, ffn_c, ffn_th, ffn_prod = (signal(n) for n in ("ffn_g", "ffn_c", "ffn_th", "ffn_prod"))
        x_final = signal("x_final")
        sin_ready, decay_th, u_zero = (signal(n) for n in ("sin_ready", "decay_th", "u_zero"))
        pe_rows = signal("pe_rows")
        ones_in = signal("ones_in")
        h_ready = signal("h_ready")

        groups = []
        start = {}

        def stage(name, *kinds):
            start[name] = len(groups)
            groups.extend(kinds)

        A8, V8, V4 = ("act", KD), ("dve", KD), ("dve", 4)
        EARLY, LATE = (4, 5), (0, 1, 2, 3, 6, 7)
        stage("attention operands", *[A8] * (8 + 10 + 8))
        stage("recurrence operands", *[A8] * 17)
        stage("gates early", *[A8, V4, A8, V4] * len(EARLY))
        stage("gates late", *[A8, V4, A8, V4] * len(LATE))
        stage("gates a", *[A8] * 8)
        stage("proj a", *[V4] * 8)
        stage("w_out", *[V8] * 8)
        stage("glu", *[A8] * 8)
        stage("sparse", *[A8] * 8)
        stage("cross kv", *[A8] * 16)
        stage("w_out_2 conv", *[V4] * 8)
        stage("w_out_2", *[V4] * 8)
        stage("cross q", *[A8] * 8)
        stage("cross o", *[V8] * 8)
        stage("ffn", *[A8] * (2 * FF))
        stage("down", *[("dve", FF)] * 8)

        def reads(who, g):
            return sum(w == who for w, _ in groups[:g + 1])

        def through(stage_, n):
            done = 0
            while done < len(stage_) and 2 * n >= sum(b for _, b in stage_[:done + 1]):
                done += 1
            return done

        def stage_groups(name, after):
            return groups[start[name]:start[after]]

        RECUR = stage_groups("recurrence operands", "gates early")
        GEARLY = stage_groups("gates early", "gates late")
        OUTB = stage_groups("w_out_2 conv", "w_out_2")
        GLATE = stage_groups("gates late", "gates a")
        nblocks = sum(n for _, n in groups)
        assert nblocks == weights.shape[0] * PB, (nblocks, weights.shape)
        NPANEL = nblocks // PB
        last_user = []
        nb = 0
        for g, (_, n) in enumerate(groups):
            nb += n
            while len(last_user) < nb // PB:
                last_user.append(g + 1)

        def window_jobs():
            jobs = []
            for b in range(NT):
                for pair in range(4):
                    kv = pair // 2
                    k0 = max(b - 1, 0) * P
                    nk = (b + 1) * P - k0
                    score = [[(memq[64 * u_:64 * u_ + 64, pair, tok(b)], skd[64 * u_:64 * u_ + 64, kv, k0:k0 + nk])]
                             for u_ in range(2)]
                    pv = [(lambda o, u_=u_: o[64 * u_:64 * u_ + 64, 0:P],
                           [(sv[:, k0 // P + s, kv * HD:kv * HD + HD], lambda pt, s=s, u_=u_: pt[:, (2 * s + u_) * P:(2 * s + u_ + 1) * P])
                            for s in range(nk // P)]) for u_ in range(2)]
                    mask = con("causal", 1) if b == 0 else con("band", 0, 2 * P)
                    jobs.append((nk, HD ** -0.5, score, mask, col("sinks", 2 * pair, 2), pv,
                                 lambda o: o[:, 0:P], yb[:, pair, tok(b)], yb[:, pair, tok(b)]))
            return jobs

        def memory_jobs():
            jobs = []
            for hd in range(4):
                for j in range(2):
                    score = [[(xq[:, hd, tok(2 * j + u_)], km[:, hd, :])] for u_ in range(2)]
                    pv = [(lambda o: o[:, 0:2 * P],
                           [(vm[:, s, tok(hd)], lambda pt, s=s: pt[:, 2 * s * P:2 * (s + 1) * P]) for s in range(2)])]
                    dst = yc[:, hd, tok(j, 2 * P)]
                    jobs.append((M, P ** -0.5, score, None, None, pv, lambda o: o[:, 0:2 * P], dst, dst))
            return jobs

        def sparse_jobs():
            jobs = []
            for b in range(NT):
                nk = (b + 1) * P
                mask = con("causal", 1) if b == 0 else sel[:, b - 1, 0:nk]
                for pair in range(4):
                    for us in ([0, 1],) if b < 2 else ([0], [1]):
                        score = [[(q2[64 * u_:64 * u_ + 64, pair, tok(b)], kd[64 * u_:64 * u_ + 64, 0:nk])] for u_ in us]
                        n = len(us)
                        pv = [(lambda o, u_=u_: o[64 * u_:64 * u_ + 64, 0:P],
                               [(vwi[:, s, 0:HD], lambda pt, s=s, i=i, n=n: pt[:, (n * s + i) * P:(n * s + i + 1) * P])
                                for s in range(nk // P)]) for i, u_ in enumerate(us)]
                        lo, hi = 64 * us[0], 64 * us[-1] + 64
                        jobs.append((nk, HD ** -0.5, score, mask, None, pv, lambda o, lo=lo, hi=hi: o[lo:hi, 0:P],
                                     mix[lo:hi, pair, tok(b)], None))
            return jobs

        def cross_jobs():
            jobs = []
            for hd in range(4):
                for j in range(2):
                    score = [[(qc[:, 2 * hd + c, tok(2 * j + u_)], k2[:, 2 * hd + c, :]) for c in range(2)] for u_ in range(2)]
                    pv = [(lambda o, c=c: o[:, 2 * c * P:2 * (c + 1) * P],
                           [(v2[:, s, tok(2 * hd + c)], lambda pt, s=s: pt[:, 2 * s * P:2 * (s + 1) * P]) for s in range(2)])
                          for c in range(2)]
                    jobs.append((M, (2 * P) ** -0.5, score, None, None, pv,
                                 lambda o: o[:, :].rearrange("p (c t) -> p c t", c=2),
                                 oc[:, 2 * hd:2 * hd + 2, tok(j, 2 * P)], None))
            return jobs

        block = ctx.enter_context(nc.Block())

        @block.tensor
        def _(pe):
            mm = nc.tensor.matmul
            bufs = {"att": (S, Pr, PT), "sq": kk, "lo": sq}

            def slot(i):
                return bufs["lo"][:, i, :] if i < 4 else bufs["sq"][:, i - 4, :]

            def mean_square(i):
                return bufs["att"][i // 2][:, i % 2, :]

            state = {"block": 0, "group": 0, "v": 0, "a": 0, "o": 0, "sq": 0, "h": 0}
            def weight():
                b = state["block"]
                state["block"] += 1
                p = b // PB
                if b % PB == 0:
                    pe.wait_ge(panel_in[p % RING].sem, 16 * (p // RING + 1))
                return ring[:, p % RING, b % PB, :]

            def dense_bank():
                g = state["group"]
                if g >= 2:
                    who = groups[g - 2][0]
                    pe.wait_ge((dense_act if who == "act" else dense_dve).sem, reads(who, g - 2))
                return bank[g % 2]

            def end_group(last):
                dense_done.inc(last)
                state["group"] += 1

            def dense_pairs(srcs, n=T):
                o = dense_bank()
                for c, src in enumerate(srcs):
                    last = mm(o[:, 0:n], weight(), src, start=c == 0, stop=c == len(srcs) - 1)
                    if c == len(srcs) - 1:
                        end_group(last)
                    if c % 2:
                        yield

            def dense(src, kt=KD, n=T):
                for _ in dense_pairs([src[:, c, :] for c in range(kt)], n):
                    pass

            def dense_normed():
                o = dense_bank()
                for c in range(KD):
                    state["h"] += 1
                    pe.wait_ge(h_ready.sem, state["h"])
                    last = mm(o[:, :], weight(), h[:, c, :], start=c == 0, stop=c == KD - 1)
                end_group(last)

            def stream(list_of_srcs):
                for srcs in list_of_srcs:
                    yield from dense_pairs(srcs)

            def fill(work, pairs=1):
                for _ in range(pairs):
                    next(work, None)

            def finish(work):
                for _ in work:
                    pass

            def dense_tokens(src, tiles, n=P):
                o = dense_bank()
                w = [weight() for _ in range(KD)]
                for t in range(tiles):
                    for c in range(KD):
                        last = mm(o[:, t * n:(t + 1) * n], src[:, c, tok(t)], w[c][:, 0:n], start=c == 0, stop=c == KD - 1)
                end_group(last)

            def other_rows(last):
                pe_rows.inc(last)
                pe.wait_ge(pe_rows.sem, pe_rows.n)

            rings = {"v": (2, v_done, v_read), "a": (4, a_done, a_read), "o": (6, o_done, o_read)}

            def take_bank(kind):
                b0, done, read = rings[kind]
                n = state[kind]
                state[kind] += 1
                if n >= 2:
                    pe.wait_ge(read.sem, n - 1)
                return bank[b0 + n % 2]

            def norm_sums(ones, norms, tiles, n=T):
                for i in range(norms):
                    o = take_bank("a")
                    for c in range(tiles):
                        state["sq"] += 1
                        pe.wait_ge(sq_ready.sem, state["sq"])
                        s = slot(i * tiles + c)
                        last = mm(o[:, 0:n], ones, s[:, 0:n], start=c == 0, stop=c == tiles - 1)
                    a_done.inc(last)

            def single(kind, lhsT, rhs, n=T):
                o = take_bank(kind)
                rings[kind][1].inc(mm(o[:, 0:n], lhsT, rhs, start=True, stop=True))

            att = {"p": 0, "pt": 0}

            def attention(jobs, work=iter(()), rate=3):
                n = len(jobs)
                for i in range(n + 2):
                    if i < n:
                        nk, _, score, *_ = jobs[i]
                        o = take_bank("v")
                        for u_, parts in enumerate(score):
                            if u_ and parts[0][0].base_partition() != score[0][0][0].base_partition():
                                other_rows(last)
                            for c, (a, b) in enumerate(parts):
                                last = mm(o[:, u_ * nk:(u_ + 1) * nk], a, b, start=c == 0, stop=c == len(parts) - 1)
                        v_done.inc(last)
                    fill(work, rate // 3)
                    if 1 <= i <= n:
                        nk, _, score, *_ = jobs[i - 1]
                        U = len(score)
                        att["p"] += 1
                        pe.wait_ge(p_ready.sem, att["p"])
                        o = take_bank("a")
                        pbuf = bufs["att"][1][:, (att["p"] - 1) % 2]
                        for s in range(nk // P):
                            for u_ in range(U):
                                last = nc.tensor.transpose(o[:, (U * s + u_) * P:(U * s + u_ + 1) * P],
                                                           pbuf[:, u_ * nk + s * P:u_ * nk + (s + 1) * P], con("ident"))
                        a_done.inc(last)
                    fill(work, rate // 3)
                    if i >= 2:
                        pv = jobs[i - 2][5]
                        att["pt"] += 1
                        pe.wait_ge(pt_ready.sem, att["pt"])
                        o = take_bank("o")
                        pt = bufs["att"][2][:, (att["pt"] - 1) % 2]
                        for view, parts in pv:
                            for s, (vs, ps) in enumerate(parts):
                                last = mm(view(o), vs, ps(pt), start=s == 0, stop=s == len(parts) - 1)
                        o_done.inc(last)
                    fill(work, 1)

            pe.wait_ge(ones_in.sem, 16)
            hs = [h[:, c, :] for c in range(KD)]
            norm_sums(con("ones"), 1, KD, M)
            norm_sums(con("ones"), 1, KD)
            pe.wait_ge(norm_applied.sem, 1)
            for n in range(4):
                dense(mem, n=M)
            for n in range(4):
                dense_tokens(mem, 2)
            dense_normed()
            for n in range(4):
                dense(h)
            dense_tokens(h, NT)
            for n in range(4):
                dense(h)
            pe.wait_ge(cst_in.sem, 16)
            work = stream([hs] * 8)
            norm_sums(con("head_ones"), 4, 1)
            fill(work, 8)
            norm_sums(con("head_ones"), 1, 1)
            fill(work, 4)
            for i in range(4):
                pe.wait_ge(rope_in.sem, i + 1)
                single("v", con("rot"), memq[:, i, :])
            fill(work, 4)
            pe.wait_ge(rope_in.sem, 5)
            for s in range(2):
                single("v", con(f"dup{s}"), skn)
                single("v", con(f"rotdup{s}"), skn)
            fill(work, 4)
            norm_sums(con("ones"), 4, 1)
            fill(work, 8)
            norm_sums(con("ones"), 4, 1, M)
            finish(work)
            work = stream([hs] * 17)
            pe.wait_ge(rope_done.sem, 6)
            pe.wait_ge(norm_applied.sem, 2 + 5 + 8)
            attention(window_jobs() + memory_jobs(), work)
            finish(work)
            norm_sums(con("head_ones"), 4, 1)
            pe.wait_ge(wa2_in.sem, 16)
            pe.wait_ge(lora_ready.sem, 1)
            pe.wait_ge(o_read.sem, state["o"])
            ybs, ycs = ([y[:, c, :] for c in range(4)] for y in (yb, yc))
            work = stream([hs, ybs, hs, ycs] * len(EARLY))
            for i in range(4):
                single("a", wa2[0:64, tok(i)], lwa[0:64, :])
                single("a", wa2[64:128, tok(i)], lwa[64:128, :])
                fill(work, 6)
                pe.wait_ge(rk_ready.sem, i + 1)
                single("v", con("head_ones"), E[0])
            finish(work)
            work = stream([hs, ybs, hs, ycs] * len(LATE))
            n_gram = n_ml = n_inv = n_av = n_wu = n_mn = 0
            for t in range(NT):
                for src in (bb, kk, k, v):
                    pe.wait_ge(head_done.sem, 4)
                    o = take_bank("a")
                    for i in range(4):
                        last = nc.tensor.transpose(o[:, tok(i)], src[:, i, tok(t)], con("ident"))
                    a_done.inc(last)
                for hb in range(2):
                    heads = [(4 * hb + j, (4 * hb + j) // 2, 64 * (j % 2)) for j in range(4)]
                    for lhs, rhs in ((kk, bb), (bb, kk), (k, kk), (bb, r), (k, r)):
                        o = take_bank("v")
                        for j in (0, 2, 1, 3):
                            hd, i, p0 = heads[j]
                            if j == 1:
                                other_rows(last)
                            last = mm(o[:, tok(j)], lhs[p0:p0 + 64, i, tok(t)], rhs[p0:p0 + 64, i, tok(t)], start=True, stop=True)
                        v_done.inc(last)
                    n_gram += 3
                    pe.wait_ge(gram_ready.sem, n_gram - 1)
                    pe.wait_ge(tm_ready.sem, 4 * (t + 1))
                    o = take_bank("a")
                    for j, (hd, i, p0) in enumerate(heads):
                        last = mm(o[:, j * HD:(j + 1) * HD], AK[:, tok(j)], vT[:, tok(hd, HD)], start=True, stop=True)
                    a_done.inc(last)
                    for l in range(1, 6):
                        n_ml += 1
                        pe.wait_ge(ml_ready.sem, n_ml)
                        if l > 1:
                            pe.wait_ge(inv_ready.sem, n_inv)
                        o = take_bank("a")
                        for j in range(4):
                            last = mm(o[:, tok(j)], ML[:, n_ml % 2, tok(j)], XX[:, tok(j)], start=True, stop=True)
                        a_done.inc(last)
                        fill(work)
                        pe.wait_ge(y_ready.sem, n_ml)
                        if l < 5:
                            o = take_bank("v")
                            for j in range(4):
                                last = mm(o[:, tok(j)], XT[:, tok(j)], YT[:, tok(j)], start=True, stop=True)
                            v_done.inc(last)
                        o = take_bank("v")
                        for j in range(4):
                            last = mm(o[:, tok(j)], YT[:, tok(j)], XT[:, tok(j)], start=True, stop=True)
                        v_done.inc(last)
                        n_inv += 1
                        fill(work)
                    pe.wait_ge(inv_ready.sem, n_inv)
                    n_av += 1
                    pe.wait_ge(av_ready.sem, n_av)
                    o = take_bank("a")
                    for j, (hd, i, p0) in enumerate(heads):
                        last = mm(o[:, tok(j)], XT[:, tok(j)], aT[:, hd, :], start=True, stop=True)
                    a_done.inc(last)
                    n_wu += 1
                    pe.wait_ge(wu_ready.sem, n_wu)
                    pe.wait_ge(gram_ready.sem, 3 * n_wu)
                    o = take_bank("v")
                    for j, (hd, i, p0) in enumerate(heads):
                        last = mm(o[p0:p0 + 64, (j // 2) * P:(j // 2 + 1) * P], WU[:, j, 0:HD], RB[:, tok(j)], start=True, stop=True)
                    v_done.inc(last)
                    o = take_bank("v")
                    for j, (hd, i, p0) in enumerate(heads):
                        ov = o[p0:p0 + 64, (j // 2) * P:(j // 2 + 1) * P]
                        mm(ov, WU[:, j, HD:P], RB[:, tok(j)], start=True, stop=False)
                        last = mm(ov, vT[:, tok(hd, HD)], RK[:, tok(j)], start=False, stop=True)
                    v_done.inc(last)
                    o = take_bank("v")
                    for c in range(2):
                        cr = slice(64 * c, 64 * c + 64)
                        if c:
                            other_rows(last)
                        for j, (hd, i, p0) in enumerate(heads):
                            q0 = (c * 2 + j // 2) * HD
                            last = mm(o[p0:p0 + 64, q0:q0 + HD], WU[cr, j, 0:HD], bT[cr, tok(hd, HD)], start=True, stop=True)
                    v_done.inc(last)
                    o = take_bank("v")
                    for c in range(2):
                        cr = slice(64 * c, 64 * c + 64)
                        if c:
                            other_rows(last)
                        for j, (hd, i, p0) in enumerate(heads):
                            q0 = (c * 2 + j // 2) * HD
                            mm(o[p0:p0 + 64, q0:q0 + HD], bT[cr, tok(hd, HD)], WU[cr, j, HD:P], start=True, stop=False)
                            last = mm(o[p0:p0 + 64, q0:q0 + HD], kT[cr, tok(hd, HD)], vT[cr, tok(hd, HD)], start=False, stop=True)
                    v_done.inc(last)
                pe.wait_ge(mn_ready.sem, 2 * (t + 1))
                for c in range(2):
                    cc = 2 * t + c
                    if cc == 0:
                        continue
                    pe.wait_ge(state_ready.sem, cc)
                    s = St[:, cc % 2]
                    o = take_bank("v")
                    for hd in range(8):
                        i, p0 = hd // 2, 64 * (hd % 2)
                        last = mm(o[p0:p0 + 64, i * C:(i + 1) * C], s[p0:p0 + 64, i * HD:(i + 1) * HD],
                                  r[p0:p0 + 64, i, tok(cc, C)], start=True, stop=True)
                    v_done.inc(last)
                    if cc < 7:
                        o = take_bank("v")
                        for hd in range(8):
                            i, p0 = hd // 2, 64 * (hd % 2)
                            last = mm(o[p0:p0 + 64, i * HD:(i + 1) * HD], MT[p0:p0 + 64, c, i * HD:(i + 1) * HD],
                                      s[p0:p0 + 64, i * HD:(i + 1) * HD], start=True, stop=True)
                        v_done.inc(last)
            finish(work)
            for i in range(4):
                pe.wait_ge(lnx_ready.sem, 1)
                single("v", con("head_ones"), rwy[:, i, :])
            work = stream([hs] * 8)
            fill(work, 4)
            bufs["lo"] = gn_sq
            norm_sums(con("head_ones"), 4, 1)
            bufs["lo"] = sq
            finish(work)
            for j in range(8):
                if j == 0:
                    pe.wait_ge(norm_applied.sem, 2 + 5 + 8 + 4 + 4)
                for _ in dense_pairs([ya[:, c, :] for c in range(4)]):
                    pass
            for j in range(8):
                if j == 0:
                    pe.wait_ge(merged_ready.sem, 8)
                dense(merged)

            bufs.update(att=(S2, P2, PT2), sq=sq_hi2)
            norm_sums(con("ones"), 1, KD)
            NA = 2 + 5 + 8 + 4 + 4
            dense_normed()
            for n in range(7 + 7):
                dense(h)
            dense_tokens(h, NT, 68)
            act_count = reads("act", start["sparse"] + 6)
            pe.wait_ge(dense_act.sem, act_count)
            for i in range(4):
                single("v", con("rot2"), q2[:, i, :])
            for i in range(2):
                single("v", con("rot2"), qi[:, i, :])
            for s in range(2):
                single("v", con(f"dup{s}"), kraw)
                single("v", con(f"rot2dup{s}"), kraw)
            pe.wait_ge(rope_done.sem, 6 + 8)
            for t in range(SEL):
                nk = (2 + t) * P
                for hd in range(4):
                    p0 = 64 * (hd % 2)
                    single("a", qi[p0:p0 + 64, hd // 2, tok(1 + t)], kid[p0:p0 + 64, 0:nk], nk)
            pe.wait_ge(conv_ready.sem, 4)
            o = take_bank("v")
            for i in range(4):
                last = mm(o[:, :], con("ones"), mix[:, 4 + i, :], start=i == 0, stop=i == 3)
            v_done.inc(last)
            norm_sums(con("ones"), 1, KD, M)
            norm_sums(con("ones"), 1, 4)
            pe.wait_ge(norm_applied.sem, NA + 2)
            for n in range(8):
                dense(mem2, n=M)
            for n in range(8):
                dense_tokens(mem2, 2)
            pe.wait_ge(mix_ready.sem, 4)
            work = stream([[mix[:, 4 + c, :] for c in range(4)]] * 8)
            attention(sparse_jobs(), work, 1)
            finish(work)
            pe.wait_ge(o_read.sem, state["o"])
            for j in range(8):
                dense(mix, 4)
            norm_sums(con("ones"), 1, KD)
            dense_normed()
            for j in range(7):
                dense(h)
            pe.wait_ge(dense_act.sem, reads("act", start["cross o"] - 1))
            attention(cross_jobs())
            pe.wait_ge(o_read.sem, state["o"])
            for j in range(8):
                dense(oc)
            norm_sums(con("ones"), 1, KD)
            dense_normed()
            for n in range(2 * FF - 1):
                dense(h)
            pe.wait_ge(ffn_prod.sem, FF)
            for j in range(8):
                dense(prod, FF)
            norm_sums(con("ones"), 1, KD)
            assert state["group"] == len(groups) and state["block"] == nblocks

        @block.scalar
        def _(act):
            fn = nc.scalar.activation
            bufs = {"att": (S, Pr, PT), "sq": kk, "lo": sq}

            def slot(i):
                return bufs["lo"][:, i, :] if i < 4 else bufs["sq"][:, i - 4, :]

            def mean_square(i):
                return bufs["att"][i // 2][:, i % 2, :]

            st = {"dense": 0, "a": 0, "norm": 0, "th": 0, "p": 0, "pt": 0, "gate": 0}
            mine = [g for g, (w, _) in enumerate(groups) if w == "act"]

            def do(ins, sig=act_chain):
                sig.inc(ins)
                act.wait_ge(sig.sem, sig.n)

            def dense_in():
                g = mine[st["dense"]]
                act.wait_ge(dense_done.sem, g + 1)
                st["dense"] += 1
                return bank[g % 2]

            def a_in():
                st["a"] += 1
                act.wait_ge(a_done.sem, st["a"])
                return bank[4 + (st["a"] - 1) % 2]

            def norms(srcs, tiles, ln_scale, eps, out_bias="zero", n=T, scales=None, refined=False, after=None):
                act.wait_ge(norm_applied.sem, st["norm"])
                for i, s in enumerate(srcs):
                    if after is not None:
                        act.wait_ge(dense_dve.sem, after + i + 1)
                    do(fn(slot(i)[:, 0:n], s, ACT.Square, scale=1.0 if scales is None else scales[i]), sq_ready)
                cnt = len(srcs) // tiles
                for i in range(cnt):
                    o = a_in()
                    if refined:
                        do(fn(mean_square(i)[:, 0:n], o[:, 0:n], ACT.Identity, bias=eps, scale=ln_scale))
                    do(fn(slot(i)[:, 0:n], o[:, 0:n], ACT.Ln, bias=eps, scale=ln_scale), a_read)
                for i in range(cnt):
                    do(fn(slot(i)[:, 0:n], slot(i)[:, 0:n], ACT.Exp, bias=col(out_bias), scale=-0.5), rinv_ready)
                st["norm"] += cnt

            def silu_in(dst):
                o = dense_in()
                n = st["th"]
                if n >= 2:
                    act.wait_ge(silu_done.sem, n - 1)
                do(fn(dst, o[:, :], ACT.Copy, scale=0.5))
                do(fn(thz[:, n % 2], o[:, :], ACT.Tanh, scale=0.5), th_ready)
                dense_act_inc()
                st["th"] += 1

            def dense_act_inc():
                act.sem_inc(dense_act.sem, 1)
                dense_act.n += 1

            def copy_dense(dst, src, **kw):
                do(fn(dst, src, ACT.Copy, **kw), dense_act)

            def raw_tile(n):
                o = dense_in()
                if n >= 2:
                    act.wait_ge(raw_used.sem, n)
                do(fn(raw[:, n % 2, 1:T + 1], o[:, :], ACT.Copy), raw_ready)
                dense_act_inc()

            def gate():
                o = dense_in()
                n = st["gate"]
                st["gate"] += 1
                if n >= 2:
                    act.wait_ge(gate_used.sem, n - 1)
                do(fn(gt[n % 2], o[:, :], ACT.Tanh, scale=0.5), dense_act)

            def read_through(reading, stage_, pairs):
                while reading["done"] < through(stage_, pairs):
                    if stage_[reading["done"]][0] == "act":
                        reading["todo"].pop(0)()
                    reading["done"] += 1

            def attention(jobs, stage_=(), todo=(), rate=3):
                n = len(jobs)
                reading = {"done": 0, "todo": list(todo)}
                for i in range(n + 1):
                    read_through(reading, stage_, rate * (i - 1))
                    if i < n:
                        nk, scale, score, mask, sinks, *_ = jobs[i]
                        st["p"] += 1
                        act.wait_ge(bias_ready.sem, st["p"])
                        s = (st["p"] - 1) % 2
                        sbuf, pbuf, _ = bufs["att"]
                        for u_ in range(len(score)):
                            if sinks is not None:
                                do(fn(small[:, s, 6 + u_:7 + u_], sinks[:, u_:u_ + 1], ACT.Exp, bias=small[:, s, 2 + u_:3 + u_], scale=1.0))
                            do(fn(pbuf[:, s, u_ * nk:(u_ + 1) * nk], sbuf[:, s, u_ * nk:(u_ + 1) * nk], ACT.Exp,
                                  bias=small[:, s, 2 + u_:3 + u_], scale=scale, accum_out=small[:, s, 4 + u_:5 + u_]),
                               exp_done if u_ == len(score) - 1 else act_chain)
                    if i >= 1:
                        nk, _, score, *_ = jobs[i - 1]
                        o = a_in()
                        st["pt"] += 1
                        if st["pt"] > 2:
                            act.wait_ge(o_done.sem, st["pt"] - 2)
                        w = len(score) * nk
                        do(fn(bufs["att"][2][:, (st["pt"] - 1) % 2, 0:w], o[:, 0:w], ACT.Copy), pt_ready)
                        a_read_inc()
                read_through(reading, stage_, 4 * len(stage_))

            def a_read_inc():
                act.sem_inc(a_read.sem, 1)
                a_read.n += 1

            act.dma_start(cols[:, :], cols_d).then_inc(cols_in.sem, 16)
            act.dma_start(mem, memt).then_inc(mem_in.sem, 16)
            act.dma_start(cst[:, 0:P], cst_d[:, 0:P]).then_inc(ones_in.sem, 16)
            act.dma_start(tmp[:, 0].bitcast(i32), pos_d).then_inc(pos_in.sem, 16)
            act.dma_start(cst[:, P:NCST], cst_d[:, P:NCST]).then_inc(cst_in.sem, 16)
            act.dma_start(wa2, wa2_d).then_inc(wa2_in.sem, 16)
            act.wait_ge(cols_in.sem, 16)
            act.wait_ge(mem_in.sem, 16)
            norms([mem[:, i, :] for i in range(KD)], KD, 1.0 / D, col("eps6"), n=M)
            for i in range(4):
                act.wait_ge(x_in[i].sem, 16)
            norms([x[:, i, :] for i in range(KD)], KD, 1.0 / D, col("eps6"))
            act.wait_ge(trig_ready.sem, 1)
            do(fn(trig[:, :, :], trig[:, :, :], ACT.Sin), sin_ready)
            for n in range(4):
                copy_dense(km[:, n, :], dense_in()[:, 0:M])
            for n in range(4):
                copy_dense(vm[:, :, tok(n)], dense_in()[:, 0:M].rearrange("p (s d) -> p s d", s=2))
            for n in range(4):
                copy_dense(memq[:, n], dense_in()[:, :])
            copy_dense(skn, dense_in()[:, :])
            copy_dense(sv, dense_in()[:, :].rearrange("p (s d) -> p s d", s=NT))
            for n in range(4):
                copy_dense(xq[:, n], dense_in()[:, :])
            norms([memq[:, i, :] for i in range(4)], 1, 1.0 / HD, col("eps6"), refined=True)
            for n in range(2):
                silu_in(yb[:, n])
            norms([skn], 1, 1.0 / HD, col("eps6"), refined=True)
            for n in range(2, 4):
                silu_in(yb[:, n])
            silu_in(yc[:, 0])
            norms([xq[:, i, :] for i in range(4)], 1, 1.0 / P, col("eps6"), refined=True)
            for n in range(1, 3):
                silu_in(yc[:, n])
            norms([km[:, i, :] for i in range(4)], 1, 1.0 / P, col("eps6"), n=M, refined=True)
            silu_in(yc[:, 3])
            act.wait_ge(raw_used.sem, 1)
            attention(window_jobs() + memory_jobs(), RECUR,
                      [lambda n=n: silu_in(ya[:, n]) for n in range(4)] + [lambda n=n: raw_tile(n) for n in range(13)])
            act.wait_ge(raw_used.sem, 1 + 13)
            norms([k[:, i, :] for i in range(4)], 1, 2.0 ** LN_SHIFT, col("kk_eps"), "kk_bias", scales=[col("k_k", i) for i in range(4)])
            do(fn(lwa[0:64, :], lwa[0:64, :], ACT.Tanh), lora_ready)
            act.wait_ge(halves.sem, 1)
            reading = {"done": 0, "todo": [gate] * (2 * len(EARLY))}
            for i in range(4):
                if i:
                    act.wait_ge(head_done.sem, i)
                o = a_in()
                do(fn(E[0], o[:, :], ACT.Tanh, bias=col("w0", i, of=half), scale=0.5), decay_th)
                a_read_inc()
                o = a_in()
                do(fn(E[5], o[:, :], ACT.Tanh, bias=col("a0", i, of=half), scale=0.5), decay_th)
                a_read_inc()
                act.wait_ge(decay_ready.sem, i + 1)
                do(fn(E[1], E[2], ACT.Exp))
                do(fn(E[4], E[2], ACT.Exp, scale=-1.0))
                do(fn(E[3], E[3], ACT.Exp))
                do(fn(gexp[:, i, 0:7], gexp[:, i, 0:7], ACT.Exp), exps_ready)
                read_through(reading, GEARLY, 6 * i)
            read_through(reading, GEARLY, 24)
            act.wait_ge(head_done.sem, 4)
            reading = {"done": 0, "todo": [gate] * (2 * len(LATE))}
            level = 0
            act.wait_ge(o_read.sem, 24)
            for t in range(NT):
                if t:
                    act.wait_ge(mn_ready.sem, 2 * t)
                for dst in (bT, aT[:, :, 0:HD], kT, vT):
                    o = a_in()
                    src = o[:, :] if dst is not None and len(dst.shape) == 2 else o[:, :].rearrange("p (h d) -> p h d", h=8)
                    do(fn(dst, src, ACT.Copy), tm_ready)
                    a_read_inc()
                for hb in range(2):
                    o = a_in()
                    do(fn(aT[:, 4 * hb:4 * hb + 4, HD:P], o[:, 0:4 * HD].rearrange("p (h d) -> p h d", h=4), ACT.Copy), av_ready)
                    a_read_inc()
                    for l in range(1, 6):
                        o = a_in()
                        do(fn(YT, o[:, :], ACT.Copy), y_ready)
                        a_read_inc()
                        read_through(reading, GLATE, 2 * level)
                        level += 1
                    o = a_in()
                    if 2 * t + hb:
                        act.wait_ge(mn_ready.sem, 2 * t + hb)
                    do(fn(WU, o[:, :].rearrange("p (h d) -> p h d", h=4), ACT.Copy), wu_ready)
                    a_read_inc()
            read_through(reading, GLATE, 6 * 12)
            act.wait_ge(lnx_ready.sem, 5)
            bufs["lo"] = gn_sq
            norms([rwy[:, i, :] for i in range(4)], 1, 1.0 / HD, col("eps_lnx"))
            bufs["lo"] = sq
            for j in range(8):
                do(fn(gates_a[:, j, :], dense_in()[:, :], ACT.Tanh, scale=0.5), dense_act)
            bufs.update(att=(S2, P2, PT2), sq=sq_hi2)
            norms([x[:, i, :] for i in range(KD)], KD, 1.0 / D, col("eps6"), after=reads("dve", start["w_out"] - 1))
            for i in range(4):
                if i >= 2:
                    act.wait_ge(u_ready.sem, i - 1)
                do(fn(thg[:, i % 2], dense_in()[:, :], ACT.Tanh, scale=0.5), dense_act)
                do(fn(ga[:, i % 2], dense_in()[:, :], ACT.Copy), glu_ready)
                dense_act_inc()
            act.wait_ge(trig_ready.sem, 2)
            do(fn(trig[:, :, :], trig[:, :, :], ACT.Sin), sin_ready)
            for i in range(4):
                copy_dense(q2[:, i], dense_in()[:, :])
            copy_dense(kraw, dense_in()[:, :])
            for i in range(2):
                copy_dense(qi[:, i], dense_in()[:, :])
            copy_dense(vwi, dense_in()[:, 0:NT * 68].rearrange("p (t d) -> p t d", t=NT))
            for t in range(SEL):
                nk = (2 + t) * P
                for hd in range(4):
                    n = 4 * t + hd
                    o = a_in()
                    if n >= 2:
                        act.wait_ge(rel_used.sem, n - 1)
                    do(fn(rel[:, n % 2, 0:nk], o[:, 0:nk], ACT.Relu, scale=HD ** -0.5), rel_ready)
                    a_read_inc()
            act.wait_ge(mem2_in.sem, 16)
            norms([mem2[:, i, :] for i in range(KD)], KD, 1.0 / D, col("eps6"), n=M)
            act.wait_ge(conv_ready.sem, 8)
            norms([mix[:, 4 + i, :] for i in range(4)], 4, 1.0 / 512, col("eps6"))
            for i in range(4):
                act.wait_ge(conv_ready.sem, 9 + i)
                do(fn(tmp[:, i], mix[:, 4 + i, :], ACT.Tanh, bias=col("ln_b_b", i, of=half), scale=col("ln_b_g", i, of=half)), conv_th)
            for n in range(8):
                copy_dense(k2[:, n, :], dense_in()[:, 0:M])
            for n in range(8):
                copy_dense(v2[:, :, tok(n)], dense_in()[:, 0:M].rearrange("p (s d) -> p s d", s=2))
            attention(sparse_jobs())
            norms([x[:, i, :] for i in range(KD)], KD, 1.0 / D, col("eps6"), after=reads("dve", start["w_out_2"] - 1))
            for j in range(8):
                copy_dense(qc[:, j], dense_in()[:, :])
            attention(cross_jobs())
            norms([x[:, i, :] for i in range(KD)], KD, 1.0 / D, col("eps6"), after=reads("dve", start["cross o"] - 1))
            act.wait_ge(ffn_c.sem, 1)
            for f in range(FF + 1):
                if f < FF:
                    o = dense_in()
                    if f >= 2:
                        act.wait_ge(ffn_c.sem, f)
                    do(fn(gpad[:, f % 2, 2:T + 2], o[:, :], ACT.Copy), ffn_g)
                    dense_act_inc()
                if f >= 1:
                    act.wait_ge(ffn_c.sem, f + 1)
                    do(fn(thf[:, (f - 1) % 2], cv[:, (f - 1) % 2], ACT.Tanh, scale=0.5), ffn_th)
                if f < FF:
                    if f >= 2:
                        act.wait_ge(ffn_prod.sem, f - 1)
                    copy_dense(upr[:, f % 2], dense_in()[:, :])
            norms([x[:, i, :] for i in range(KD)], KD, 1.0 / D, col("eps6"), after=reads("dve", start["down"] - 1))

        @block.vector
        def _(dve):
            V = nc.vector
            bufs = {"att": (S, Pr, PT), "sq": kk, "lo": sq}

            def slot(i):
                return bufs["lo"][:, i, :] if i < 4 else bufs["sq"][:, i - 4, :]

            def mean_square(i):
                return bufs["att"][i // 2][:, i % 2, :]

            st = {"dense": 0, "v": 0, "gate": 0, "o": 0, "rinv": 0, "att": 0, "exp": 0}
            mine = [g for g, (w, _) in enumerate(groups) if w == "dve"]

            def do(ins, sig=dve_chain):
                sig.inc(ins)
                dve.wait_ge(sig.sem, sig.n)

            def signal_now(sig):
                dve.sem_inc(sig.sem, 1)
                sig.n += 1

            def tt(out, a, b, op, sig=dve_chain):
                do(V.tensor_tensor(out, a, b, op), sig)

            def ts(out, a, s1, s2, o0, o1, sig=dve_chain):
                do(V.tensor_scalar(out, a, s1, s2, o0, o1), sig)

            def ts1(out, a, s1, o0, sig=dve_chain):
                do(V.tensor_scalar(out, a, s1, None, o0), sig)

            def stt(out, a, s, b, o0, o1, sig=dve_chain):
                do(V.scalar_tensor_tensor(out=out, in0=a, scalar=s, in1=b, op0=o0, op1=o1), sig)

            def copy(out, a, sig=dve_chain):
                do(V.tensor_copy(out, a), sig)

            def v_in():
                st["v"] += 1
                dve.wait_ge(v_done.sem, st["v"])
                return bank[2 + (st["v"] - 1) % 2]

            def dense_in():
                g = mine[st["dense"]]
                dve.wait_ge(dense_done.sem, g + 1)
                st["dense"] += 1
                return bank[g % 2]

            def gated(j, more):
                g = mine[st["dense"]]
                n = st["gate"]
                st["gate"] += 1
                dve.wait_ge(dense_act.sem, reads("act", g - 1))
                o = dense_in()
                stt(tmp[:, 2] if more else partial[j], gt[n % 2], 1.0, o[:, :], ADD, MUL, dense_dve)
                signal_now(gate_used)
                if more:
                    tt(partial[j], partial[j], tmp[:, 2], ADD)

            def read_through(reading, stage_, pairs):
                while reading["done"] < through(stage_, pairs):
                    f = reading["todo"].pop(0)
                    if f is not None:
                        f()
                    reading["done"] += 1

            def gated_todo(tiles):
                return [f for j in tiles for f in (None, lambda j=j: gated(j, False), None, lambda j=j: gated(j, True))]

            def rinv_in(i, n=T):
                st["rinv"] += 1
                dve.wait_ge(rinv_ready.sem, st["rinv"])
                return slot(i)[:, 0:n]

            def rinv_refined(i, n=T):
                y = rinv_in(i, n)
                t = tmp[:, 0, 0:n]
                tt(t, y, y, MUL)
                tt(t, t, mean_square(i)[:, 0:n], MUL)
                ts(t, t, -0.5, 1.5, MUL, ADD)
                tt(t, t, y, MUL)
                return t

            def angles(src, name, sig, which):
                dve.wait_ge(src.sem, 16)
                copy(tmp[:, 1], tmp[:, 0].bitcast(i32))
                if which:
                    dve.wait_ge(rope_done.sem, 6)
                ts1(tmp[:, 1], tmp[:, 1], col(name), MUL)
                for c in range(2):
                    ts(tmp[:, 2], tmp[:, 1], 1 / (2 * math.pi), 0.25 * c, MUL, ADD)
                    ts(tmp[:, 2], tmp[:, 2], ROUND, ROUND, ADD, SUB)
                    a = tmp[:, 1]
                    for part in TWO_PI:
                        stt(tmp[:, 3], tmp[:, 2], -part, a, MUL, ADD)
                        a = tmp[:, 3]
                    if c:
                        ts1(tmp[:, 3], tmp[:, 3], col("half_pi"), ADD)
                    ts(trig[:, c], tmp[:, 3], math.pi - 4e-7, -math.pi + 4e-7, MIN, MAX, sig if c else dve_chain)

            def apply_norm(g, n=T, tiles=KD, src=x, dst=h):
                ri = rinv_in(0, n)
                for i in range(tiles):
                    stt(dst[:, i, :], src[:, i, :], col(g, i), ri, MUL, MUL, h_ready if dst is h else dve_chain)
                signal_now(norm_applied)

            def rope(dst, src):
                tt(tmp[:, 0], src, trig[:, 1], MUL)
                o = v_in()
                tt(tmp[:, 1], o[:, :], trig[:, 0], MUL, v_read)
                tt(dst, tmp[:, 0], tmp[:, 1], ADD, rope_done)

            def rope_dup(dst):
                o = v_in()
                tt(tmp[:, 0], o[:, :], trig[:, 1], MUL, v_read)
                o = v_in()
                tt(tmp[:, 1], o[:, :], trig[:, 0], MUL, v_read)
                tt(dst, tmp[:, 0], tmp[:, 1], ADD, rope_done)

            def attention(jobs, stage_=(), todo=(), rate=3):
                n = len(jobs)
                reading = {"done": 0, "todo": list(todo)}
                for i in range(n + 2):
                    if i >= 1:
                        read_through(reading, stage_, rate * (i - 1))
                    if i < n:
                        nk, scale, score, mask, sinks, *_ = jobs[i]
                        U = len(score)
                        w = U * nk
                        o = v_in()
                        s = st["att"] % 2
                        st["att"] += 1
                        sc_ = bufs["att"][0][:, s, 0:w]
                        sc3 = sc_.rearrange("p (u n) -> p u n", u=U)
                        if mask is None:
                            copy(sc_, o[:, 0:w], v_read)
                        else:
                            tt(sc3, o[:, 0:w].rearrange("p (u n) -> p u n", u=U),
                               mask.unsqueeze(1).broadcast_to([P, U, nk]), ADD, v_read)
                        mx, nb_ = small[:, s, 0:U], small[:, s, 2:2 + U]
                        do(V.reduce_max(mx, sc3, AX))
                        if sinks is None:
                            ts1(nb_, mx, -scale, MUL, bias_ready)
                        else:
                            stt(mx, mx, scale, sinks, MUL, MAX)
                            ts1(nb_, mx, -1.0, MUL, bias_ready)
                    if 1 <= i <= n:
                        nk, scale, score, mask, sinks, *_ = jobs[i - 1]
                        U = len(score)
                        s = st["exp"] % 2
                        st["exp"] += 1
                        dve.wait_ge(exp_done.sem, st["exp"])
                        den = small[:, s, 4:4 + U]
                        if sinks is not None:
                            tt(den, den, small[:, s, 6:6 + U], ADD)
                        do(V.reciprocal(small[:, s, 8:8 + U], den))
                        for u_ in range(U):
                            pb = bufs["att"][1][:, s, u_ * nk:(u_ + 1) * nk]
                            ts1(pb, pb, small[:, s, 8 + u_:9 + u_], MUL, p_ready if u_ == U - 1 else dve_chain)
                    if i >= 2:
                        _, _, _, _, _, _, view, dst, gate = jobs[i - 2]
                        st["o"] += 1
                        dve.wait_ge(o_done.sem, st["o"])
                        o = view(bank[6 + (st["o"] - 1) % 2])
                        if gate is None:
                            copy(dst, o, o_read)
                        else:
                            tt(dst, o, gate, MUL, o_read)
                read_through(reading, stage_, 4 * len(stage_))

            dve.wait_ge(cols_in.sem, 16)
            ts1(half[:, :], cols[:, :], 0.5, MUL, halves)
            for s in range(2):
                do(V.memset(raw[:, s, 0:1], 0.0), raw_used if s else dve_chain)
            angles(pos_in, "freq", trig_ready, 0)
            dve.wait_ge(mem_in.sem, 16)
            apply_norm("mem_norm_g", M, KD, mem, mem)
            for i in range(4):
                dve.wait_ge(x_in[i].sem, 16)
            apply_norm("norm_g")
            for i in range(4):
                ri = rinv_refined(i)
                stt(memq[:, i, :], memq[:, i, :], col("q_g"), ri, MUL, MUL, norm_applied)
                signal_now(rope_in)
            ri = rinv_refined(0)
            stt(skn, skn, col("k_g"), ri, MUL, MUL, norm_applied)
            signal_now(rope_in)
            dve.wait_ge(sin_ready.sem, 1)
            for i in range(4):
                rope(memq[:, i, :], memq[:, i, :])
            for s in range(2):
                rope_dup(skd[:, s, :])
            for i in range(4):
                ri = rinv_refined(i)
                stt(xq[:, i, :], xq[:, i, :], col("xq_g"), ri, MUL, MUL, norm_applied)
            for i in range(4):
                ri = rinv_refined(i, M)
                stt(km[:, i, :], km[:, i, :], col("xk_g"), ri, MUL, MUL, norm_applied)
            dve.wait_ge(silu_done.sem, 8)

            def shifted(n):
                dve.wait_ge(raw_ready.sem, n + 1)
                cur, prev = raw[:, n % 2, 1:T + 1], raw[:, n % 2, 0:T]
                m, dst = (12, lwa) if n == 0 else [(4, k), (0, r), (8, v)][(n - 1) // 4]
                if n:
                    m, dst = m + (n - 1) % 4, dst[:, (n - 1) % 4, :]
                else:
                    dve.wait_ge(silu_done.sem, 12)
                tt(tmp[:, 2], prev, cur, SUB)
                stt(dst, tmp[:, 2], col("mu", m), cur, MUL, ADD, raw_used)

            attention(window_jobs() + memory_jobs(), RECUR, [None] * 4 + [lambda n=n: shifted(n) for n in range(13)])
            for i in range(4):
                ri = rinv_in(i)
                ts1(tmp[:, 0], ri, 1e12, MIN)
                stt(kk[:, i, :], k[:, i, :], col("k_k", i), tmp[:, 0], MUL, MUL, norm_applied)
            reading = {"done": 0, "todo": gated_todo(EARLY)}
            for i in range(4):
                dve.wait_ge(decay_th.sem, 2 * i + 1)
                half_decay = -0.5 * EXP_HALF
                ts(E[0], E[0], half_decay, half_decay, MUL, ADD)
                dve.wait_ge(cst_in.sem, 16)
                do(V.tensor_tensor_scan(E[1], con("restart", 0, T), E[0], 0.0, MUL, ADD))
                sums = E[1].rearrange("p (c t) -> p c t", t=C)
                tt(gexp[:, i, 0:7], sums[:, 0:7, C - 1], sums[:, 0:7, C // 2 - 1], SUB)
                tt(gexp[:, i, 0:7], gexp[:, i, 0:7], sums[:, 1:8, C // 2 - 1], ADD)
                tt(E[2].rearrange("p (c t) -> p c t", t=C), sums, sums[:, :, C // 2 - 1:C // 2].broadcast_to([P, T // C, C]), SUB)
                dve.wait_ge(decay_th.sem, 2 * i + 2)
                tt(E[3], E[2], E[0], SUB, decay_ready)
                ts(E[5], E[5], 0.5, 0.5, MUL, ADD)
                ts(tmp[:, 0], E[5], -1.0, col("k_a", i), ADD, MUL)
                stt(k[:, i, :], tmp[:, 0], 1.0, k[:, i, :], ADD, MUL)
                stt(E[0], r[:, i, :], col("r_k", i), k[:, i, :], MUL, MUL, rk_ready)
                tt(bb[:, i, :], kk[:, i, :], E[5], MUL)
                dve.wait_ge(exps_ready.sem, i + 1)
                stt(kk[:, i, :], kk[:, i, :], -1.0, E[3], MUL, MUL)
                tt(bb[:, i, :], bb[:, i, :], E[4], MUL)
                tt(k[:, i, :], k[:, i, :], E[4], MUL)
                tt(r[:, i, :], r[:, i, :], E[1], MUL)
                read_through(reading, GEARLY, 6 * i)
                o = v_in()
                tt(bonus[:, i, :], o[:, :], v[:, i, :], MUL, v_read)
                signal_now(head_done)
            read_through(reading, GEARLY, 24)
            reading = {"done": 0, "todo": gated_todo(LATE)}
            level = 0
            for t in range(NT):
                for hb in range(2):
                    j4 = "p (j t) -> p j t"
                    b4 = [P, 4, P]
                    if 2 * t + hb:
                        dve.wait_ge(wu_ready.sem, 2 * t + hb)
                    lev = con("level0").unsqueeze(1).broadcast_to(b4)
                    levT = con("levelT", 0).unsqueeze(1).broadcast_to(b4)
                    strict = con("strictT").unsqueeze(1).broadcast_to(b4)
                    incl = con("inclT").unsqueeze(1).broadcast_to(b4)
                    eye = con("ident").unsqueeze(1).broadcast_to(b4)

                    def f4(a):
                        return a.rearrange(j4, j=4)
                    o = v_in()
                    tt(f4(tmp[:, 0]), f4(o[:, :]), lev, MUL, v_read)
                    tt(f4(XX), f4(tmp[:, 0]), eye, ADD)
                    o = v_in()
                    tt(f4(tmp[:, 0]), f4(o[:, :]), levT, MUL)
                    if 2 * t + hb:
                        dve.wait_ge(ml_ready.sem, 5 * (2 * t + hb))
                    tt(f4(AB), f4(o[:, :]), strict, MUL, v_read)
                    tt(f4(XT), f4(tmp[:, 0]), eye, ADD, gram_ready)
                    o = v_in()
                    tt(f4(AK), f4(o[:, :]), strict, MUL, v_read)
                    signal_now(gram_ready)
                    o = v_in()
                    tt(f4(RB), f4(o[:, :]), incl, MUL, v_read)
                    o = v_in()
                    tt(f4(RK), f4(o[:, :]), incl, MUL, v_read)
                    signal_now(gram_ready)
                    for l in range(1, 6):
                        if l < 5:
                            o = v_in()
                            tt(XX, XX, o[:, :], ADD, v_read)
                        o = v_in()
                        tt(XT, XT, o[:, :], ADD, v_read)
                        signal_now(inv_ready)
                        read_through(reading, GLATE, 2 * level)
                        level += 1
                    rs = r[:, 2 * hb:2 * hb + 2, tok(t)]
                    o = v_in()
                    tt(rs, rs, o[:, 0:2 * P].rearrange("p (i t) -> p i t", i=2), ADD, v_read)
                    o = v_in()
                    copy(rwy[:, 2 * hb:2 * hb + 2, tok(t)], o[:, 0:2 * P].rearrange("p (i t) -> p i t", i=2), v_read)
                    o = v_in()
                    eye64 = con("ident64", 0, HD).unsqueeze(1).broadcast_to([P, 4, HD])
                    tt(tmp[:, 1, 0:4 * HD].rearrange("p (q d) -> p q d", q=4), o[:, 0:4 * HD].rearrange("p (q d) -> p q d", q=4), eye64, ADD, v_read)
                    mt = MT[:, :, 2 * hb * HD:2 * (hb + 1) * HD]
                    copy(mt, tmp[:, 1, 0:4 * HD].rearrange("p (c d) -> p c d", c=2))
                    o = v_in()
                    copy(NN[:, :, 2 * hb * HD:2 * (hb + 1) * HD], o[:, 0:4 * HD].rearrange("p (c d) -> p c d", c=2), v_read)
                    signal_now(mn_ready)
                for c in range(2):
                    cc = 2 * t + c
                    src = NN[:, c]
                    if cc:
                        o = v_in()
                        ys = rwy[:, :, tok(cc, C)]
                        tt(ys, ys, o[:, 0:4 * C].rearrange("p (i t) -> p i t", i=4), ADD, v_read)
                        if cc < 7:
                            o = v_in()
                            tt(tmp[:, 2, 0:4 * HD], o[:, 0:4 * HD], NN[:, c], ADD, v_read)
                            src = tmp[:, 2, 0:4 * HD]
                    if cc < 7:
                        tt(St[:, (cc + 1) % 2].rearrange("p (i d) -> p i d", i=4), src.rearrange("p (i d) -> p i d", i=4),
                           gexp[:, :, cc:cc + 1].broadcast_to([P, 4, HD]), MUL, state_ready)
            read_through(reading, GLATE, 6 * 12)
            signal_now(lnx_ready)
            for i in range(4):
                o = v_in()
                stt(rwy[:, i, :], o[:, :], -1.0 / HD, rwy[:, i, :], MUL, ADD, v_read)
                signal_now(lnx_ready)
            bufs["lo"] = gn_sq
            for i in range(4):
                ri = rinv_in(i)
                stt(tmp[:, 0], rwy[:, i, :], col("lnx_g", i), ri, MUL, MUL)
                stt(tmp[:, 0], tmp[:, 0], col("lnx_b", i), bonus[:, i, :], ADD, ADD)
                tt(ya[:, i, :], tmp[:, 0], ya[:, i, :], MUL, norm_applied)
            bufs["lo"] = sq
            for j in range(8):
                dve.wait_ge(dense_act.sem, reads("act", start["gates a"] + j))
                o = dense_in()
                stt(tmp[:, 0], gates_a[:, j, :], 1.0, o[:, :], ADD, MUL, dense_dve)
                tt(merged[:, j, :], tmp[:, 0], partial[j], ADD, merged_ready)

            def add_tile(j, s=1.0):
                o = dense_in()
                stt(x[:, j, :], o[:, :], s, x[:, j, :], MUL, ADD, dense_dve)

            def add_dense(s=1.0):
                for j in range(KD):
                    add_tile(j, s)

            add_dense(0.5)
            signal_now(block1_done)

            bufs.update(att=(S2, P2, PT2), sq=sq_hi2)
            for s in range(4):
                do(V.memset(u[:, s, 0:TAPS - 1], 0.0), u_zero if s == 3 else dve_chain)
            apply_norm("norm_mix_g")
            angles(pos2_in, "freq2", trig_ready, 1)
            for i in range(4):
                dve.wait_ge(u_ready.sem, i + 1)
                acc = mix[:, 4 + i, :]
                ts(acc, u[:, i, 0:T], col("conv_w", i * TAPS), col("conv_b", i), MUL, ADD)
                for w in range(1, TAPS):
                    stt(acc, u[:, i, w:w + T], col("conv_w", i * TAPS + w), acc, MUL, ADD,
                        conv_ready if w == TAPS - 1 else dve_chain)
            dve.wait_ge(sin_ready.sem, 2)
            dve.wait_ge(dense_act.sem, reads("act", start["cross kv"] - 1))
            for i in range(4):
                rope(q2[:, i, :], q2[:, i, :])
            for i in range(2):
                rope(qi[:, i, :], qi[:, i, :])
            rope_dup(kd)
            rope_dup(kid)
            for t in range(NT):
                ts1(vwi[:, t, HD:HD + 4], vwi[:, t, HD:HD + 4], 0.5, MUL)
            for t in range(SEL):
                nk = (2 + t) * P
                for hd in range(4):
                    n = 4 * t + hd
                    dve.wait_ge(rel_ready.sem, n + 1)
                    w = vwi[:, 1 + t, HD + hd:HD + hd + 1]
                    if hd == 0:
                        ts1(sc[:, t, 0:nk], rel[:, n % 2, 0:nk], w, MUL, rel_used)
                    else:
                        stt(sc[:, t, 0:nk], rel[:, n % 2, 0:nk], w, sc[:, t, 0:nk], MUL, ADD, rel_used)
                tt(sc[:, t, nk - P:nk], sc[:, t, nk - P:nk], con("causal", 1), ADD)
            o = v_in()
            copy(tmp[:, 0], o[:, :], v_read)
            for i in range(4):
                stt(mix[:, 4 + i, :], tmp[:, 0], -1.0 / 512, mix[:, 4 + i, :], MUL, ADD, conv_ready)
            dve.wait_ge(mem2_in.sem, 16)
            apply_norm("norm_mem_g", M, KD, mem2, mem2)
            ri = rinv_in(0)
            for i in range(4):
                tt(mix[:, 4 + i, :], mix[:, 4 + i, :], ri, MUL, conv_ready)
            signal_now(norm_applied)
            for i in range(4):
                dve.wait_ge(conv_th.sem, i + 1)
                ts(mix[:, 4 + i, :], mix[:, 4 + i, :], col("ln_b_g", i, of=half), col("ln_b_b", i, of=half), MUL, ADD)
                stt(mix[:, 4 + i, :], tmp[:, i], 1.0, mix[:, 4 + i, :], ADD, MUL, mix_ready)
            for rnd in range(TOPK // 8):
                for t in range(SEL):
                    nk = (2 + t) * P
                    do(V.max(max8[:, t, :], sc[:, t, 0:nk]))
                    do(V.match_replace(sc[:, t, 0:nk], max8[:, t, :], sc[:, t, 0:nk], TAKEN))
            for t in range(SEL):
                nk = (2 + t) * P
                ts(sel[:, t, 0:nk], sc[:, t, 0:nk], -3e38, MASKED, ALU.is_gt, MUL)
            attention(sparse_jobs(), OUTB, [lambda j=j: add_tile(j) for j in range(KD)], 1)
            add_dense()
            apply_norm("norm_cross_g")
            attention(cross_jobs())
            add_dense()
            apply_norm("norm_ffn_g")
            do(V.memset(gpad[:, :, 0:FTAPS - 1], 0.0), ffn_c)
            for f in range(FF + 1):
                if f < FF:
                    dve.wait_ge(ffn_g.sem, f + 1)
                    s = f % 2
                    ts(cv[:, s], gpad[:, s, 0:T], col("ffn_w", f * FTAPS), col("ffn_b", f), MUL, ADD)
                    stt(cv[:, s], gpad[:, s, 1:T + 1], col("ffn_w", f * FTAPS + 1), cv[:, s], MUL, ADD)
                    stt(cv[:, s], gpad[:, s, 2:T + 2], col("ffn_w", f * FTAPS + 2), cv[:, s], MUL, ADD, ffn_c)
                if f >= 1:
                    s = (f - 1) % 2
                    dve.wait_ge(ffn_th.sem, f)
                    stt(tmp[:, 0], thf[:, s], 1.0, cv[:, s], ADD, MUL)
                    dve.wait_ge(dense_act.sem, reads("act", start["ffn"] - 1) + 2 * f)
                    tt(prod[:, f - 1, :], tmp[:, 0], upr[:, s], MUL, ffn_prod)
            add_dense(0.5)
            ri = rinv_in(0)
            for i in range(KD):
                stt(h[:, i, :], x[:, i, :], col("norm_final_g", i), ri, MUL, MUL, x_final)

        @block.gpsimd
        def _(pool):
            G = nc.gpsimd

            def do(ins, sig=pool_chain):
                sig.inc(ins)
                pool.wait_ge(sig.sem, sig.n)

            dst = [y[:, n] for y in (yb, yc, ya) for n in range(4)]
            for n in range(12):
                pool.wait_ge(th_ready.sem, n + 1)
                do(G.tensor_scalar(thz[:, n % 2], thz[:, n % 2], 1.0, None, ADD))
                do(G.tensor_tensor(dst[n], dst[n], thz[:, n % 2], MUL), silu_done)
            n = 0
            for t in range(NT):
                for hb in range(2):
                    pool.wait_ge(gram_ready.sem, 3 * (2 * t + hb) + 1)
                    for l in range(1, 6):
                        n += 1
                        if n > 2:
                            pool.wait_ge(y_ready.sem, n - 2)
                        lev = con("levelT", l).unsqueeze(1).broadcast_to([P, 4, P])
                        do(G.tensor_tensor(ML[:, n % 2].rearrange("p (j t) -> p j t", j=4), AB.rearrange("p (j t) -> p j t", j=4), lev, MUL), ml_ready)
            pool.wait_ge(block1_done.sem, 1)
            pool.dma_start(tmp[:, 0].bitcast(i32), pos2_d).then_inc(pos2_in.sem, 16)
            pool.dma_start(mem2, mem2t).then_inc(mem2_in.sem, 16)
            pool.wait_ge(u_zero.sem, 1)
            for i in range(4):
                pool.wait_ge(glu_ready.sem, i + 1)
                do(G.tensor_scalar(thg[:, i % 2], thg[:, i % 2], 0.5, 0.5, MUL, ADD))
                do(G.tensor_tensor(u[:, i, TAPS - 1:TAPS - 1 + T], thg[:, i % 2], ga[:, i % 2], MUL), u_ready)


        @block.sync
        def _(sp):
            for i in range(4):
                sp.dma_start(x[:, 2 * i:2 * i + 2, :], xt[:, 2 * i:2 * i + 2, :]).then_inc(x_in[i].sem, 16)
            for p in range(NPANEL):
                if p >= RING:
                    sp.wait_ge(dense_done.sem, last_user[p - RING])
                sp.dma_start(ring[:, p % RING], weights[p]).then_inc(panel_in[p % RING].sem, 16)
            for i in range(KD):
                sp.wait_ge(x_final.sem, i + 1)
                sp.dma_start(out_d[:, i, :], h[:, i, :]).then_inc(out_done.sem, 16)
            sp.wait_ge(out_done.sem, 16 * KD)


def kernel(**inputs):
    import concourse.bacc as bacc
    from concourse.bass_utils import run_bass_kernel_spmd

    a = {n: np.asarray(v) for n, v in inputs.items()}

    def tiles(m):
        return np.ascontiguousarray(m.T.reshape(-1, P, m.shape[0]).transpose(1, 0, 2))

    def blocks(w, order=None):
        k, n = w.shape
        b = w.reshape(k // P, P, n // P, P).transpose(2, 0, 1, 3)
        return b if order is None else b[order]

    w_in, w_in2 = blocks(a["w_in"][0]), a["w_in_2"][0]
    q, kp, vp, qip, kip, wip, glu = np.split(w_in2, np.cumsum([512, 64, 64, 256, 64, 4]), axis=1)
    pad = np.zeros((D, 60), np.float32)
    w_in2 = blocks(np.concatenate([q, kp, kip, qip, vp, wip, pad], 1))
    ga, gg = blocks(glu[:, :512]), blocks(glu[:, 512:])
    pa, pb, pc = (blocks(a[n][0]) for n in ("w_proj_a", "w_proj_b", "w_proj_c"))
    parts = [blocks(a["w_mem_kv"][0]), w_in[17:23], w_in[27:31], w_in[23:27], w_in[31:35]]
    parts += [w_in[13:17], w_in[12], w_in[4:8], w_in[0:4], w_in[8:12]]
    for j in (4, 5, 0, 1, 2, 3, 6, 7):
        parts += [w_in[43 + j], pb[j], w_in[51 + j], pc[j]]
    parts += [w_in[35:43], pa]
    parts.append(blocks(a["w_out"][0]))
    for j in range(4):
        parts += [gg[j], ga[j]]
    parts.append(w_in2)
    parts += [blocks(a[n][0]) for n in ("w_k_cross_2", "w_v_cross_2")]
    w_out2 = blocks(a["w_out_2"][0])
    parts += [w_out2[:, 4:], w_out2[:, :4]]
    parts += [blocks(a[n][0]) for n in ("w_q_cross_2", "w_o_cross_2")]
    wg, wu = blocks(a["w_gate_2"][0]), blocks(a["w_up_2"][0])
    for f in range(FF):
        parts += [wg[f], wu[f]]
    parts.append(blocks(a["w_down_2"][0]))
    stream = np.concatenate([p.reshape(-1, P, P) for p in parts])
    weights = np.ascontiguousarray(stream.reshape(-1, PB, P, P).transpose(0, 2, 1, 3))

    cols = np.zeros((P, NCOLS), np.float32)

    def put(name, v):
        o, n = COLS[name]
        cols[:, o:o + n] = v

    def per_feature(v):
        return v.reshape(-1, P).T

    for name in ("norm_g", "mem_norm_g", "w0", "a0", "k_k", "k_a", "lnx_g", "lnx_b"):
        put(name, per_feature(a[name][0]))
    put("mu", per_feature(np.concatenate([a["mu_rkv"][0].reshape(-1), a["mu_wa"][0].reshape(-1)])))
    put("r_k", per_feature(a["r_k"][0].reshape(-1)))
    for name, src in (("q_g", "q_norm_g"), ("k_g", "k_norm_g")):
        put(name, np.tile(a[src][0], 2)[:, None])
    put("xq_g", a["xq_norm_g"][0][:, None])
    put("xk_g", a["xk_norm_g"][0][:, None])
    put("sinks", np.broadcast_to(a["sinks"][0], (P, 8)))
    for name in ("norm_mix_g", "norm_cross_g", "norm_mem_g", "norm_ffn_g", "ln_b_g", "ln_b_b"):
        put(name, per_feature(a[name + "_2"][0]))
    put("norm_final_g", per_feature(a["norm_final_g_2"]))
    put("conv_w", a["conv_b_w_2"][0].T.reshape(4, P, TAPS).transpose(1, 0, 2).reshape(P, -1))
    put("conv_b", per_feature(a["conv_b_b_2"][0]))
    put("ffn_w", a["ffn_conv_w_2"][0].T.reshape(FF, P, FTAPS).transpose(1, 0, 2).reshape(P, -1))
    put("ffn_b", per_feature(a["ffn_conv_b_2"][0]))
    d = np.arange(P) % HD
    put("freq", (10000.0 ** (-(d % 32) / 32))[:, None])
    put("freq2", np.where(d < 16, 500000.0 ** (-2.0 * (d % 8) / 16), 0.0)[:, None])
    for name, value in (("eps6", 1e-6), ("eps_lnx", 64e-5), ("kk_eps", 2.0 ** -64),
                        ("kk_bias", LN_SHIFT / 2 * math.log(2)), ("half_pi", math.pi / 2)):
        put(name, value)

    arrays = {
        "xt": tiles(a["x"][0]), "memt": tiles(a["mem"][0]), "mem2t": tiles(a["mem_2"][0]),
        "weights": weights, "cols_in": cols, "cst_in": constants(),
        "wa2": np.ascontiguousarray(np.concatenate([a["w2"][0], a["a2"][0]])),
        "pos": np.ascontiguousarray(np.broadcast_to(a["positions"], (P, T))),
        "pos2": np.ascontiguousarray(np.broadcast_to(a["positions_2"], (P, T))),
    }
    nc = bacc.Bacc("TRN2", target_bir_lowering=False, num_devices=1)
    aps = [nc.dram_tensor(n, v.shape, mybir.dt.from_np(v.dtype), kind="ExternalInput").ap() for n, v in arrays.items()]
    out = nc.dram_tensor("out", (P, KD, T), mybir.dt.float32, kind="ExternalOutput").ap()
    build(nc, *aps, out)
    res = run_bass_kernel_spmd(nc, [arrays], core_ids=[0]).results[0]["out"]
    return np.ascontiguousarray(res.transpose(1, 0, 2).reshape(D, T).T)[None]
```
